# Optimizing a Trainium2 kernel written in Bass

```python
import jax
import jax.numpy as jnp
from jax import lax
import numpy as np

D_MODEL = 1024
BATCH = 1
SEQ = 256
DEPTH = 1

MEM_LEN = 256
NORM_EPS = 1e-6

A_GROUPS = ((128, 1), (512, 4), (2048, 16))
A_N_GROUPS = len(A_GROUPS)
A_HEADS = 4
A_HEAD_DIM = 128
A_WIDTH = A_HEADS * A_HEAD_DIM
BLOCK = 128

R_HEAD = 64
R_HEADS = 8
R_WIDTH = R_HEADS * R_HEAD
R_DECAY_LORA = 64
R_AAA_LORA = 64
R_GATE_LORA = 128
R_GN_EPS = 64e-5

C_HEADS = 4
C_HEAD_DIM = 128
C_WIDTH = C_HEADS * C_HEAD_DIM

ROPE_THETA = 500000.0
ROT_DIM = A_HEAD_DIM // 4

N_BRANCH = 3
BRANCH_WIDTH = 512

N_EXPERTS = 32
TOP_K = 4
D_FF = D_MODEL
SWIGLU_ALPHA = 1.702
SWIGLU_LIMIT = 7.0
MOE_ROWS = 256

A_QKV_COLS = A_N_GROUPS * A_WIDTH
R_COLS = 3 * R_WIDTH + R_DECAY_LORA + R_AAA_LORA + R_GATE_LORA
R_SPLITS = (R_WIDTH, 2 * R_WIDTH, 3 * R_WIDTH, 3 * R_WIDTH + R_DECAY_LORA,
            3 * R_WIDTH + R_DECAY_LORA + R_AAA_LORA)
GATE_COLS = N_BRANCH * D_MODEL
OFF_AQ = 0
OFF_AK = OFF_AQ + A_QKV_COLS
OFF_AV = OFF_AK + A_QKV_COLS
OFF_R = OFF_AV + A_QKV_COLS
OFF_CQ = OFF_R + R_COLS
OFF_GATE = OFF_CQ + C_WIDTH
IN_COLS = OFF_GATE + GATE_COLS

kernel_name = 'hybrid_dilated_rwkv7_memxattn_moe_layer'

def rms_norm(t, gain, eps=NORM_EPS):
    tf = t.astype(jnp.float32)
    y = tf * lax.rsqrt(jnp.mean(tf * tf, axis=-1, keepdims=True) + eps)
    return (y * gain.astype(jnp.float32)).astype(t.dtype)

def partial_rotary(t, positions):
    half = ROT_DIM // 2
    inv_freq = ROPE_THETA ** (-jnp.arange(half, dtype=jnp.float32) / half)
    ang = positions.astype(jnp.float32)[..., None] * inv_freq
    ang = ang.reshape(ang.shape[:2] + (1,) * (t.ndim - 3) + (half,))
    cos, sin = jnp.cos(ang), jnp.sin(ang)
    tf = t.astype(jnp.float32)
    t1, t2, rest = tf[..., :half], tf[..., half:ROT_DIM], tf[..., ROT_DIM:]
    out = jnp.concatenate([t1 * cos - t2 * sin, t2 * cos + t1 * sin, rest], axis=-1)
    return out.astype(t.dtype)

def banded_causal_attention(q, k, v, span):
    n, length, heads, dh = q.shape
    n_blk = -(-length // BLOCK)
    pad = n_blk * BLOCK - length
    qp = jnp.pad(q, ((0, 0), (0, pad), (0, 0), (0, 0)))
    kp = jnp.pad(k, ((0, 0), (span, pad), (0, 0), (0, 0)))
    vp = jnp.pad(v, ((0, 0), (span, pad), (0, 0), (0, 0)))
    scale = dh ** -0.5
    qi = jnp.arange(BLOCK)[:, None]
    ki = jnp.arange(BLOCK + span)[None, :]
    rel = qi + span - ki

    def one_block(blk):
        s0 = blk * BLOCK
        qb = lax.dynamic_slice_in_dim(qp, s0, BLOCK, axis=1)
        kb = lax.dynamic_slice_in_dim(kp, s0, BLOCK + span, axis=1)
        vb = lax.dynamic_slice_in_dim(vp, s0, BLOCK + span, axis=1)
        s = jnp.einsum('nqhd,nkhd->nhqk', qb, kb, preferred_element_type=jnp.float32) * scale
        valid = (rel >= 0) & (rel <= span) & (s0 - span + ki >= 0)
        s = jnp.where(valid, s, -jnp.inf)
        m = jnp.max(s, axis=-1, keepdims=True)
        p = jnp.exp(s - m)
        denom = jnp.sum(p, axis=-1, keepdims=True)
        o = jnp.einsum('nhqk,nkhd->nqhd', p, vb.astype(jnp.float32))
        o = o / jnp.transpose(denom, (0, 2, 1, 3))
        lse = jnp.swapaxes((m + jnp.log(denom))[..., 0], 1, 2)
        return o.astype(q.dtype), lse

    o, lse = lax.map(one_block, jnp.arange(n_blk))
    o = jnp.moveaxis(o, 0, 1).reshape(n, n_blk * BLOCK, heads, dh)[:, :length]
    lse = jnp.moveaxis(lse, 0, 1).reshape(n, n_blk * BLOCK, heads)[:, :length]
    return o, lse

def dilated_attention(q, k, v, window, dilation):
    b, s, h, dh = q.shape
    sub = s // dilation

    def to_residues(t):
        return t.reshape(b, sub, dilation, h, dh).transpose(0, 2, 1, 3, 4).reshape(b * dilation, sub, h, dh)

    o, lse = banded_causal_attention(to_residues(q), to_residues(k), to_residues(v), window // dilation)
    o = o.reshape(b, dilation, sub, h, dh).transpose(0, 2, 1, 3, 4).reshape(b, s, h, dh)
    lse = lse.reshape(b, dilation, sub, h).transpose(0, 2, 1, 3).reshape(b, s, h)
    return o, lse

def dilated_mixture_attention(zq, zk, zv, q_gain, k_gain, positions):
    b, s, _ = zq.shape
    shape = (b, s, A_N_GROUPS, A_HEADS, A_HEAD_DIM)
    q = partial_rotary(rms_norm(zq.reshape(shape), q_gain), positions)
    k = partial_rotary(rms_norm(zk.reshape(shape), k_gain), positions)
    v = zv.reshape(shape)
    outs, lses = [], []
    for g, (window, dilation) in enumerate(A_GROUPS):
        o, l = dilated_attention(q[:, :, g], k[:, :, g], v[:, :, g], window, dilation)
        outs.append(o)
        lses.append(l)
    alpha = jax.nn.softmax(jnp.stack(lses, axis=0), axis=0)
    out = jnp.einsum('gbsh,gbshd->bshd', alpha, jnp.stack(outs, axis=0).astype(jnp.float32))
    return out.reshape(b, s, A_WIDTH).astype(zq.dtype)

def rwkv7_step(state, inp):
    r_t, w_t, k_t, v_t, a_t, b_t = inp
    sa = jnp.einsum('bhvk,bhk->bhv', state, a_t)
    state = state * w_t[:, :, None, :] + sa[..., None] * b_t[:, :, None, :] + v_t[..., None] * k_t[:, :, None, :]
    y = jnp.einsum('bhvk,bhk->bhv', state, r_t)
    return state, y

def rwkv7_time_mix(zr, mu, w0, w2, a0, a2, g2, k_k, k_a, r_k, ln_w, ln_b):
    b, s, _ = zr.shape
    f32 = jnp.float32
    prev = jnp.pad(zr, ((0, 0), (1, 0), (0, 0)))[:, :-1]
    zr = zr + (prev - zr) * mu
    r, k, v, w_lo, a_lo, g_lo = jnp.split(zr, R_SPLITS, axis=-1)
    w = -jax.nn.softplus(-(w0 + jnp.tanh(w_lo) @ w2)) - 0.5
    decay = jnp.exp(-jnp.exp(w.astype(f32)))
    a = jax.nn.sigmoid(a0 + a_lo @ a2)
    g = jax.nn.sigmoid(g_lo) @ g2
    heads = lambda t: t.reshape(b, s, R_HEADS, R_HEAD).astype(f32)
    kk = heads(k * k_k)
    kk = kk / jnp.maximum(jnp.sqrt(jnp.sum(kk * kk, axis=-1, keepdims=True)), 1e-12)
    k = k * (1.0 + (a - 1.0) * k_a)
    r_h, k_h, v_h, a_h, w_h = heads(r), heads(k), heads(v), heads(a), heads(decay)
    seq_first = lambda t: jnp.moveaxis(t, 1, 0)
    xs = (seq_first(r_h), seq_first(w_h), seq_first(k_h), seq_first(v_h), seq_first(-kk), seq_first(kk * a_h))
    state0 = jnp.zeros((b, R_HEADS, R_HEAD, R_HEAD), f32)
    _, y = lax.scan(rwkv7_step, state0, xs)
    y = jnp.moveaxis(y, 0, 1)
    mean = jnp.mean(y, axis=-1, keepdims=True)
    var = jnp.mean(jnp.square(y - mean), axis=-1, keepdims=True)
    y = ((y - mean) * lax.rsqrt(var + R_GN_EPS)).reshape(b, s, R_WIDTH)
    y = y * ln_w.astype(f32) + ln_b.astype(f32)
    bonus = jnp.sum(r_h * k_h * r_k.astype(f32), axis=-1, keepdims=True) * v_h
    y = (y + bonus.reshape(b, s, R_WIDTH)) * g.astype(f32)
    return y.astype(zr.dtype)

def memory_cross_attention(zq, mem_n, w_mem_kv, q_gain, k_gain):
    b, s, _ = zq.shape
    m = mem_n.shape[1]
    q = rms_norm(zq.reshape(b, s, C_HEADS, C_HEAD_DIM), q_gain)
    k, v = jnp.split(mem_n @ w_mem_kv, 2, axis=-1)
    k = rms_norm(k.reshape(b, m, C_HEADS, C_HEAD_DIM), k_gain)
    v = v.reshape(b, m, C_HEADS, C_HEAD_DIM)
    sc = jnp.einsum('bshd,bmhd->bhsm', q, k, preferred_element_type=jnp.float32) * (C_HEAD_DIM ** -0.5)
    p = jax.nn.softmax(sc, axis=-1)
    o = jnp.einsum('bhsm,bmhd->bshd', p, v.astype(jnp.float32))
    return o.reshape(b, s, C_WIDTH).astype(zq.dtype)

def moe_ffn(h, router_w, router_b, w1, b1, w2, b2):
    b, s, d = h.shape
    n_tok = b * s
    n_assign = n_tok * TOP_K
    xt = h.reshape(n_tok, d)
    logits = (xt @ router_w + router_b).astype(jnp.float32)
    top_val, top_idx = lax.top_k(logits, TOP_K)
    gate = jax.nn.softmax(top_val, axis=-1)
    flat_e = top_idx.reshape(-1)
    flat_g = gate.reshape(-1)
    flat_tok = jnp.arange(n_assign, dtype=jnp.int32) // TOP_K
    order = jnp.argsort(flat_e)
    sorted_e = flat_e[order]
    counts = jnp.bincount(flat_e, length=N_EXPERTS)
    padded = (counts + MOE_ROWS - 1) // MOE_ROWS * MOE_ROWS
    pad_end = jnp.cumsum(padded)
    pad_start = pad_end - padded
    raw_start = jnp.cumsum(counts) - counts
    dest = pad_start[sorted_e] + jnp.arange(n_assign, dtype=jnp.int32) - raw_start[sorted_e]
    n_blocks = -(-n_assign // MOE_ROWS) + N_EXPERTS
    n_rows = n_blocks * MOE_ROWS
    row_tok = jnp.full((n_rows,), n_tok, jnp.int32).at[dest].set(flat_tok[order])
    row_gate = jnp.zeros((n_rows,), jnp.float32).at[dest].set(flat_g[order])
    block_expert = jnp.minimum(
        jnp.searchsorted(pad_end, jnp.arange(n_blocks, dtype=jnp.int32) * MOE_ROWS, side='right'),
        N_EXPERTS - 1)
    x_pad = jnp.concatenate([xt, jnp.zeros((1, d), xt.dtype)], axis=0)

    def expert_block(args):
        tok, e = args
        u = x_pad[tok] @ w1[e] + b1[e]
        glu = jnp.minimum(u[:, :D_FF], SWIGLU_LIMIT)
        lin = jnp.clip(u[:, D_FF:], -SWIGLU_LIMIT, SWIGLU_LIMIT)
        act = glu * jax.nn.sigmoid(SWIGLU_ALPHA * glu) * (lin + 1.0)
        return act @ w2[e] + b2[e]

    y_rows = lax.map(expert_block, (row_tok.reshape(n_blocks, MOE_ROWS), block_expert))
    y_rows = y_rows.reshape(n_rows, d).astype(jnp.float32) * row_gate[:, None]
    y = jax.ops.segment_sum(y_rows, row_tok, num_segments=n_tok + 1)[:n_tok]
    return y.reshape(b, s, d).astype(h.dtype)

def setup_inputs(seed: int = 0) -> dict:
    key = jax.random.key(seed)
    ks = iter(jax.random.split(key, 40))
    L, D = DEPTH, D_MODEL

    def nrm(shape, scale):
        return scale * jax.random.normal(next(ks), shape, jnp.float32)

    x = nrm((BATCH, SEQ, D), 1.0)
    mem = nrm((BATCH, MEM_LEN, D), 1.0)
    positions = (jnp.arange(SEQ, dtype=jnp.int32)[None, :]
                 + jax.random.randint(next(ks), (BATCH, 1), 0, 4096, dtype=jnp.int32))
    norm_mix = 1.0 + nrm((L, D), 0.02)
    w_in = nrm((L, D, IN_COLS), D ** -0.5)
    b_gate = nrm((L, GATE_COLS), 0.02)
    a_q_gain = 1.0 + nrm((L, A_HEAD_DIM), 0.02)
    a_k_gain = 1.0 + nrm((L, A_HEAD_DIM), 0.02)
    r_mu = jax.random.uniform(next(ks), (L, R_COLS), jnp.float32, 0.0, 1.0)
    r_w0 = jnp.broadcast_to(jnp.linspace(-6.0, -1.0, R_WIDTH, dtype=jnp.float32), (L, R_WIDTH)) + nrm((L, R_WIDTH), 0.1)
    r_w2 = nrm((L, R_DECAY_LORA, R_WIDTH), 0.1 * R_DECAY_LORA ** -0.5)
    r_a0 = nrm((L, R_WIDTH), 0.1)
    r_a2 = nrm((L, R_AAA_LORA, R_WIDTH), 0.1 * R_AAA_LORA ** -0.5)
    r_g2 = nrm((L, R_GATE_LORA, R_WIDTH), R_GATE_LORA ** -0.5)
    r_k_k = 0.85 + nrm((L, R_WIDTH), 0.02)
    r_k_a = 1.0 + nrm((L, R_WIDTH), 0.02)
    r_r_k = nrm((L, R_HEADS, R_HEAD), 0.1)
    r_ln_w = 1.0 + nrm((L, R_WIDTH), 0.02)
    r_ln_b = nrm((L, R_WIDTH), 0.01)
    mem_norm = 1.0 + nrm((L, D), 0.02)
    w_mem_kv = nrm((L, D, 2 * C_WIDTH), D ** -0.5)
    c_q_gain = 1.0 + nrm((L, C_HEAD_DIM), 0.02)
    c_k_gain = 1.0 + nrm((L, C_HEAD_DIM), 0.02)
    w_branch = nrm((L, N_BRANCH, BRANCH_WIDTH, D), BRANCH_WIDTH ** -0.5)
    w_out = nrm((L, D, D), D ** -0.5)
    norm_ffn = 1.0 + nrm((L, D), 0.02)
    router_w = nrm((L, D, N_EXPERTS), D ** -0.5)
    router_b = nrm((L, N_EXPERTS), 0.01)
    exp_w1 = nrm((L, N_EXPERTS, D, 2 * D_FF), D ** -0.5)
    exp_b1 = nrm((L, N_EXPERTS, 2 * D_FF), 0.01)
    exp_w2 = nrm((L, N_EXPERTS, D_FF, D), D_FF ** -0.5)
    exp_b2 = nrm((L, N_EXPERTS, D), 0.01)
    return {'x': x, 'mem': mem, 'positions': positions, 'norm_mix': norm_mix, 'w_in': w_in,
            'b_gate': b_gate, 'a_q_gain': a_q_gain, 'a_k_gain': a_k_gain, 'r_mu': r_mu,
            'r_w0': r_w0, 'r_w2': r_w2, 'r_a0': r_a0, 'r_a2': r_a2, 'r_g2': r_g2,
            'r_k_k': r_k_k, 'r_k_a': r_k_a, 'r_r_k': r_r_k, 'r_ln_w': r_ln_w, 'r_ln_b': r_ln_b,
            'mem_norm': mem_norm, 'w_mem_kv': w_mem_kv, 'c_q_gain': c_q_gain, 'c_k_gain': c_k_gain,
            'w_branch': w_branch, 'w_out': w_out, 'norm_ffn': norm_ffn, 'router_w': router_w,
            'router_b': router_b, 'exp_w1': exp_w1, 'exp_b1': exp_b1, 'exp_w2': exp_w2, 'exp_b2': exp_b2}

def reference(x, mem, positions, norm_mix, w_in, b_gate, a_q_gain, a_k_gain, r_mu, r_w0, r_w2,
              r_a0, r_a2, r_g2, r_k_k, r_k_a, r_r_k, r_ln_w, r_ln_b, mem_norm, w_mem_kv,
              c_q_gain, c_k_gain, w_branch, w_out, norm_ffn, router_w, router_b,
              exp_w1, exp_b1, exp_w2, exp_b2):
    b, s, d = x.shape
    for l in range(DEPTH):
        h = rms_norm(x, norm_mix[l])
        z = h @ w_in[l]
        y_a = dilated_mixture_attention(z[..., OFF_AQ:OFF_AK], z[..., OFF_AK:OFF_AV],
                                        z[..., OFF_AV:OFF_R], a_q_gain[l], a_k_gain[l], positions)
        y_b = rwkv7_time_mix(z[..., OFF_R:OFF_CQ], r_mu[l], r_w0[l], r_w2[l], r_a0[l], r_a2[l],
                             r_g2[l], r_k_k[l], r_k_a[l], r_r_k[l], r_ln_w[l], r_ln_b[l])
        y_c = memory_cross_attention(z[..., OFF_CQ:OFF_GATE], rms_norm(mem, mem_norm[l]),
                                     w_mem_kv[l], c_q_gain[l], c_k_gain[l])
        gates = jax.nn.sigmoid(z[..., OFF_GATE:] + b_gate[l]).reshape(b, s, N_BRANCH, d)
        branches = jnp.stack([y_a, y_b, y_c], axis=2)
        proj = jnp.einsum('bsnc,ncd->bsnd', branches, w_branch[l])
        merged = jnp.sum(gates * proj, axis=2)
        x = x + merged @ w_out[l]
        x = x + moe_ffn(rms_norm(x, norm_ffn[l]), router_w[l], router_b[l],
                        exp_w1[l], exp_b1[l], exp_w2[l], exp_b2[l])
    return x


_drawn_inputs = setup_inputs


def setup_inputs(seed=0):
    import zlib

    import numpy as np

    out = dict(_drawn_inputs(seed))
    spreads = {}
    factors = {'b_gate': 8.0,
     'a_q_gain': 25.075,
     'a_k_gain': 18.478,
     'r_w2': 30.386,
     'r_ln_w': 24.968,
     'r_ln_b': 34.264,
     'mem_norm': 8.0,
     'c_q_gain': 8.0,
     'c_k_gain': 3.782,
     'exp_b1': 40.335,
     'exp_b2': 46.792,
     'r_a0': 4.872,
     'r_a2': 5.52,
     'r_k_k': 8.0,
     'r_k_a': 8.0,
     'r_r_k': 3.207,
     'norm_ffn': 5.831,
     'router_b': 8.0}
    for name, (base, spread) in spreads.items():
        noise = np.random.default_rng([zlib.crc32(name.encode()), seed]).standard_normal(out[name].shape)
        drawn = base * np.exp(spread * noise) if base else spread * noise
        out[name] = jnp.asarray(drawn.astype(out[name].dtype))
    for name, factor in factors.items():
        out[name] = (out[name] * factor).astype(out[name].dtype)
    return out
```

```python
import math
from contextlib import ExitStack

import concourse.bass as bass
from concourse import mybir
from concourse.alu_op_type import AluOpType as ALU
import numpy as np

F32 = mybir.dt.float32
I32 = mybir.dt.int32
ACT = mybir.ActivationFunctionType
AX = mybir.AxisListType.X

P = 128
D = 1024
T = 256
NT = T // P
KC = D // P
W = 512
HEADS, HD = 4, 128
GROUPS = ((128, 1), (512, 4), (2048, 16))
NG = len(GROUPS)
MEM = 256
RH, RD = 8, 64
PAIRS = RH // 2
CH = 64
NCH = T // CH
LEVELS = 6
NM = PAIRS * NCH
E, TOPK, DFF = 32, 4, 1024
CAP = 64
ROT = HD // 4
HALF = ROT // 2
THETA = 500000.0
EPS = 1e-6
GN_EPS = 64e-5
ALPHA, LIMIT = 1.702, 7.0
SCALE = HD ** -0.5
NEG = -1e30
LOGC = -math.exp(-0.5)
UNSEL = 1000.0

A_COLS = NG * HEADS * HD
OFF_R = 3 * A_COLS
R_COLS = 3 * RH * RD + 2 * 64 + 128
OFF_CQ = OFF_R + R_COLS
OFF_GATE = OFF_CQ + W

ROWS = {}
for _n, _c in (("norm_mix", 8), ("b_gate", 24), ("r_mu", 14), ("r_w0", 4), ("r_a0", 4), ("r_k_k", 4), ("r_k_a", 4),
               ("r_r_k", 4), ("r_ln_w", 4), ("r_ln_b", 4), ("mem_norm", 8), ("norm_ffn", 8)):
    ROWS[_n] = (sum(c for _, c in ROWS.values()), _c)
NROWS = sum(c for _, c in ROWS.values())

CONST = {}
for _n, _c in (("ident", 128), ("jblk", 128), ("amask", NG * 256), ("strict", CH), ("incl", CH), ("level", LEVELS * CH),
               ("eye", CH), ("reset", T), ("earlier", 128), ("ones", 128), ("iota", CAP), ("invf", HALF)):
    CONST[_n] = (sum(c for _, c in CONST.values()), _c)
NCONST = sum(c for _, c in CONST.values())

ORDER = [("vec", 0), ("normx", 0), ("rz", 0), ("angle", 0), ("rz", 1), ("rz", 2), ("rz", 3), ("lora", 0), ("normm", 0), ("ck", 0),
         ("kk", 0), ("cv", 0), ("cq", 0), ("bonus", 0), ("tilde", 0), ("attn_s", 3), ("gates_c0", 0), ("attn_t", 3),
         ("gates", 2), ("tok", 0), ("L", 0), ("az", 0), ("inv", 0), ("inv", 1), ("inv", 2), ("attn_s", 0), ("inv", 3),
         ("attn_t", 0), ("inv", 4), ("inv", 5), ("az", 1), ("seq", 0), ("seq", 1), ("attn_s", 1), ("seq", 2),
         ("attn_t", 1), ("seq", 3), ("gn", 0), ("az", 2), ("gn2", 0), ("attn_s", 2), ("gates", 1), ("attn_t", 2),
         ("outA", 0), ("gates", 0), ("wo", 0)]
ORDER = [o for o in ORDER if o[0] != "gates_c0"]
NORMS = ["x", "mem"] + [("ck", t) for t in range(NT)] + [("cq", t) for t in range(NT)] + \
    [(k, g, t) for g in range(NG) for k in "qk" for t in range(NT)] + ["ffn"]


def weight_loads():
    out = [("r", i) for i in range(4)] + [("mk", 0), ("mv", 0), ("cq", 0)]
    for st, a in ORDER:
        if st == "az":
            out += [("aq", a), ("ak", a), ("av", a)]
        if st == "gates":
            out += [("wb", a), ("g0", a), ("g1", a)]
    return out + [("wo", 0), ("wo", 1)]


RING = 4
SLOTS = 6


def build(nc, A, out):
    ctx = ExitStack()
    with ctx:
        def sb(name, shape, dt=F32):
            return ctx.enter_context(nc.sbuf_tensor(name, shape, dt))

        sems = {}

        def S(name):
            if name not in sems:
                sems[name] = ctx.enter_context(nc.semaphore(name))
            return sems[name]

        ring = sb("ring", [P, SLOTS, 4096])
        const = sb("const", [P, NCONST])
        gains = sb("gains", [P, 4, HD])
        x = sb("x", [P, NT, D])
        hT = sb("hT", [P, KC, T])
        A1 = sb("A1", [P, 6, 1024])
        PP = sb("PP", [P, 3072])
        yT = sb("yT", [P, HEADS, T])
        merged = sb("merged", [P, KC, T])
        EA = sb("EA", [P, 8, 1024])
        vecT = sb("vecT", [P, NROWS])
        ajunk = sb("ajunk", [P, W])
        omm = sb("omm", [P, 14])
        omka = sb("omka", [P, 4])
        ssq = sb("ssq", [P, 80])
        rst = sb("rst", [P, 80])
        negh = sb("negh", [P, 16])
        trig = sb("trig", [P, NT, 2 * ROT])
        rotb = sb("rotb", [P, 2, HEADS, ROT])
        posi = sb("posi", [P, NT], I32)
        posf = sb("posf", [P, NT])
        ePT = sb("ePT", [P, PAIRS, NCH])
        mx = sb("mx", [P, 6, NT, HEADS])
        lsum = sb("lsum", [P, 2, NT, HEADS])
        flag = sb("flag", [P, 4])
        flagi = sb("flagi", [P, 1], I32)
        small = sb("small", [P, NT, 8])
        banks = [ctx.enter_context(nc.psum_tensor(f"bank{i}", [P, W], F32)) for i in range(8)]

        def cc(name, *shape):
            a, n = CONST[name]
            return const[:, a:a + n]

        ident = cc("ident")

        def vcol(name, i=0, n=1):
            a = ROWS[name][0]
            return vecT[:, a + i:a + i + n]

        def rep(ap, n):
            return ap.unsqueeze(1).to_broadcast([ap.shape[0], n, ap.shape[1]])

        def each(ap, n):
            return ap.unsqueeze(2).to_broadcast([ap.shape[0], ap.shape[1], n])

        def row_tile(name):
            r0, n = ROWS[name]
            return rows[r0:r0 + n, :]

        def row_source(name):
            if name == "r_r_k":
                return A[name].rearrange("o (a c) b -> (o a) (c b)", c=2)
            return A[name].rearrange("o (a b) -> (o a) b", b=P)

        FA = ring[:, RING:SLOTS, :].rearrange("p a (b c) -> p (a b) c", c=1024)

        def ch(ap):
            return ap.rearrange("p (a t) -> p a t", t=T)

        def mm64(ap):
            return ap.rearrange("p (m t) -> p m t", t=CH)

        r_, k_, v_, bv = FA[:, 0, :], FA[:, 1, :], FA[:, 2, :], FA[:, 4, :]
        wag = FA[:, 3, 0:2 * T].rearrange("p (a t) -> p a t", t=T)
        w2a, g2w = EA[:, 0, 0:W], EA[:, 0, W:2 * W]
        sgw, cum, a_, g_, kk, tmp6, tmp7 = (EA[:, i, :] for i in range(1, 8))
        at_, bt_, eN = FA[:, 5, :], EA[:, 7, :], FA[:, 6, :]
        Vt, Kt, Bt = EA[:, 1, :], EA[:, 2, :], EA[:, 3, :]
        LabT, LakT, LrbT, LrkT = EA[:, 5, :], EA[:, 6, :], EA[:, 0, :], FA[:, 6, :]
        XT, X, Tm, Lm = EA[:, 7, :], FA[:, 1, :], FA[:, 2, :], FA[:, 7, :]
        stS = [FA[:, 7, 0:256], FA[:, 7, 768:1024]]
        Rb, Ub = FA[:, 7, 256:512], FA[:, 7, 512:768]
        yB = FA[:, 3, :]
        gnd, gnq, gnr = FA[:, 1, :], FA[:, 2, :], EA[:, 5, :]
        zq, zk = A1[:, 0, :].rearrange("p (t n) -> p t n", t=NT), A1[:, 1, :].rearrange("p (t n) -> p t n", t=NT)
        qT, kT = ch(A1[:, 2, :]), ch(A1[:, 3, :])
        vv, O = A1[:, 4, :].rearrange("p (t n) -> p t n", t=NT), A1[:, 5, :].rearrange("p (t n) -> p t n", t=NT)
        hx = PP[:, 0:2048].rearrange("p (t n) -> p t n", t=NT)
        memx = A1[:, 0:2, :]
        rows = A1[:, 2, 0:P]
        memT = merged
        sg = [A1[:, 0, 0:T], A1[:, 0, T:2 * T]]
        gp = [A1[:, 1, 0:T], A1[:, 1, T:2 * T]]

        loads = weight_loads()
        load_no = {n: i for i, n in enumerate(loads)}
        base = [sum(1 for i in range(len(loads)) if i % RING == s) if s < RING else 0 for s in range(SLOTS)]

        def weights(eng, name):
            i = load_no[name]
            eng.wait_ge(S(f"slot_landed{i % RING}"), 16 * (i // RING + 1))
            return ring[:, i % RING, :]

        def slot_used(ins, name):
            ins.then_inc(S(f"slot_used{load_no[name] % RING}"), 1)

        family = {"mT": "hT", "nT": "hT", "kt": "vt", "bt": "vt", "lak": "lab", "lrb": "lab", "lrk": "lab", "lw": "lora",
                  "la": "lora", "lg": "lora", "ck": "qk", "cq": "qk", "aq": "qk", "ak": "qk", "av": "cv", "ckT": "qkT",
                  "cqT": "qkT", "aqT": "qkT", "akT": "qkT", "bn": "gn", "gm": "gn", "gv": "gn"}
        ledger, by_kind, in_bank = {}, {}, []

        def Filled(kind):
            return S(f"{family.get(kind, kind)}_filled")

        def Drained(kind):
            return S(f"{family.get(kind, kind)}_drained")

        def filled(eng, kind, *idx):
            b, n = ledger[(kind, idx)]
            eng.wait_ge(Filled(kind), n)
            return banks[b]

        def drained(eng, kind, *idx):
            eng.wait_ge(Drained(kind), ledger[(kind, idx)][1])

        def tile_parts(g):
            full = [(t, p, 2 * p, 2, 256, 0) for t in range(NT) for p in range(2)]
            return full if g == NG else [(0, 0, 0, 4, 128, 0)] + full[2:]

        def prob(g, t):
            if g < NG:
                nk = 128 * (t + 1)
                pr = PP[:, 512 * t:512 * t + 4 * nk].rearrange("p (h k) -> p h k", h=HEADS)
                pt = PP[:, 1536 + 512 * t:1536 + 512 * t + 4 * nk].rearrange("p (h b k) -> p h b k", h=HEADS, k=P)
            else:
                pr = (PP[:, 0:1024] if t == 0 else A1[:, 0, :]).rearrange("p (h k) -> p h k", h=HEADS)
                pt = (PP[:, 1024:2048] if t == 0 else A1[:, 1, :]).rearrange("p (h b k) -> p h b k", h=HEADS, k=P)
            return pr, pt

        def reached(eng, name, value):
            if not isinstance(value, int) or value > 0:
                eng.wait_ge(S(name), value)

        b2s = EA[0:E, 0, :]
        b1T, b1raw = EA[:, 1, 0:W], EA[:, 1, W:2 * W]
        rw = EA[:, 2, 0:KC * E].rearrange("p (k e) -> p k e", e=E)
        rank = EA[:, 2, 256:256 + 2 * (E + 1)].rearrange("p (t e) -> p t e", t=NT)
        gate = EA[:, 2, 384:384 + 2 * (E + 1)].rearrange("p (t e) -> p t e", t=NT)
        rbias = EA[:, 2, 512:512 + E]
        lgt = EA[:, 2, 576:576 + 2 * E].rearrange("p (t e) -> p t e", t=NT)
        sel = EA[:, 2, 640:640 + 2 * E].rearrange("p (t e) -> p t e", t=NT)
        eqs = EA[:, 2, 704:704 + 2 * E].rearrange("p (t e) -> p t e", t=NT)
        cnt = EA[:, 2, 768:768 + 2 * E].rearrange("p (t e) -> p t e", t=NT)
        tie = EA[:, 2, 832:832 + 2 * E].rearrange("p (t e) -> p t e", t=NT)
        zer = EA[:, 2, 896:896 + E]
        G = EA[:, 3, 0:2 * CAP].rearrange("p (t c) -> p t c", t=NT)
        Gw = A1[:, 1, 0:4 * CAP].rearrange("p (t c) -> p t c", t=NT)
        GTw = EA[:, 3, 256:512]
        xgT = EA[:, 3, 512:1024].rearrange("p (k c) -> p k c", c=CAP)
        glu, sig = EA[:, 4, 0:W], EA[:, 4, W:2 * W]
        lin, actT = EA[:, 5, 0:W], EA[:, 5, W:2 * W]
        ysb = EA[:, 6, 0:W]
        usb = A1[:, 0, :]
        WT = EA[0:E, 7, 0:T]
        xn = hT[:, :, :].rearrange("p a b -> p (a b)").rearrange("p (t n) -> p t n", t=NT)
        hnT = PP[:, 0:2048].rearrange("p (k t) -> p k t", t=T)
        XG, U0, U1, TU, YB, C0, C1, GB = banks
        LO, HI = slice(0, CAP), slice(CAP, 2 * CAP)

        block = ctx.enter_context(nc.Block())

        @block.tensor
        def _(pe):
            mm = nc.tensor.matmul

            def claim(kind, *idx):
                b = len(in_bank) % 8
                if len(in_bank) >= 8:
                    drained(pe, in_bank[-8][0], *in_bank[-8][1])
                f = family.get(kind, kind)
                by_kind[f] = by_kind.get(f, 0) + 1
                ledger[(kind, idx)] = (b, by_kind[f])
                in_bank.append((kind, idx))
                return banks[b]

            def done(ins, kind):
                ins.then_inc(Filled(kind), 1)

            def vec(_):
                pe.wait_ge(S("ident_landed"), 16)
                pe.wait_ge(S("rows_landed"), 16 * len(ROWS))
                done(nc.tensor.transpose(claim("vec")[:, 0:NROWS], rows[0:NROWS, :], ident[0:NROWS, 0:NROWS]), "vec")

            def turn(kind, src, sem):
                for t in range(NT):
                    pe.wait_ge(S(sem), t + 1)
                    for half in range(2):
                        bank = claim(kind, t, half)
                        for j in range(4):
                            c = 4 * half + j
                            ins = nc.tensor.transpose(bank[:, j * P:(j + 1) * P], src[:, t, c * P:(c + 1) * P], ident)
                        done(ins, kind)

            def channel_chunk(bank, w, c, rhs, nk=KC, width=W):
                for kc in range(nk):
                    ins = mm(bank[:, 0:T], w[:, kc * width + c * P:kc * width + (c + 1) * P], rhs[:, kc, :],
                             start=(kc == 0), stop=(kc == nk - 1))
                return ins

            def rz(i):
                if i == 0:
                    for t in range(NT):
                        for half in range(2):
                            drained(pe, "hT", t, half)
                w = weights(pe, ("r", i))
                width = W if i < 3 else 256
                for c in range(width // P):
                    bank = claim("rz", 4 * i + c)
                    ins = channel_chunk(bank, w, c, hT, width=width)
                    done(ins, "rz")

            def lora(_):
                pe.wait_ge(S("lora_landed"), 48)
                pe.wait_ge(S("wlo_ready"), 2)
                drained(pe, "rz", 13)
                for p in range(PAIRS):
                    for kind, lhs, rhs in (("lw", w2a[0:64, p * P:(p + 1) * P], wag[0:64, 0, :]),
                                           ("la", w2a[64:128, p * P:(p + 1) * P], wag[64:128, 0, :]),
                                           ("lg", g2w[:, p * P:(p + 1) * P], wag[:, 1, :])):
                        done(mm(claim(kind, p)[:, 0:T], lhs, rhs, start=True, stop=True), kind)

            def token_tile(kind, t, src, w):
                bank = claim(kind, t)
                for kc in range(KC):
                    ins = mm(bank[:, :], src[:, kc, t * P:(t + 1) * P], w[:, kc * W:(kc + 1) * W],
                             start=(kc == 0), stop=(kc == KC - 1))
                done(ins, kind)

            def heads_turn(kind, srckind, src):
                for t in range(NT):
                    if srckind[0] == "A":
                        pe.wait_ge(S("rot_done"), srckind[1] * NT + t + 1)
                    else:
                        drained(pe, srckind[1], t)
                    bank = claim(kind, t)
                    for h in range(HEADS):
                        ins = nc.tensor.transpose(bank[:, h * P:(h + 1) * P], src[:, t, h * P:(h + 1) * P], ident)
                    done(ins, kind)

            def ck(_):
                for t in range(NT):
                    for half in range(2):
                        drained(pe, "mT", t, half)
                w = weights(pe, ("mk", 0))
                for t in range(NT):
                    token_tile("ck", t, memT, w)

            def cv(_):
                w = weights(pe, ("mv", 0))
                for t in range(NT):
                    token_tile("cv", t, memT, w)

            def cq(_):
                w = weights(pe, ("cq", 0))
                for t in range(NT):
                    token_tile("cq", t, hT, w)
                heads_turn("ckT", ("C", "ck"), zk)
                heads_turn("cqT", ("C", "cq"), zq)

            def kkn(_):
                pe.wait_ge(S("const_landed"), 16)
                for half in range(2):
                    pe.wait_ge(S("kksq_ready"), half + 1)
                    done(mm(claim("kn", half)[:, :], cc("jblk"), tmp6[:, half * W:(half + 1) * W], start=True, stop=True), "kn")

            def bonus(_):
                pe.wait_ge(S("rkk_ready"), 1)
                for half in range(2):
                    done(mm(claim("bn", half)[:, :], cc("jblk"), tmp6[:, half * W:(half + 1) * W], start=True, stop=True), "bn")

            def head64(bank, col, pairs_of):
                for j, (lhs, rhs, n, first, last) in enumerate(pairs_of):
                    for h in range(2):
                        s = slice(64 * h, 64 * h + 64)
                        ins = mm(bank[s, col:col + n], lhs[s, :], rhs[s, :], start=first, stop=last,
                                 skip_group_check=True)
                return ins

            def tok(_):
                pe.wait_ge(S("tilde_ready"), 1)
                for kind, src in (("vt", v_), ("kt", k_), ("bt", bt_)):
                    for half in range(2):
                        bank = claim(kind, half)
                        for m in range(8):
                            c = half * W + m * CH
                            ins = head64(bank, m * CH, [(src[:, c:c + CH], cc("eye"), CH, m == 0, m == 7)])
                        done(ins, kind)

            def L(_):
                for kind, lhs, rhs in (("lab", bt_, at_), ("lak", k_, at_), ("lrb", bt_, r_), ("lrk", k_, r_)):
                    for half in range(2):
                        bank = claim(kind, half)
                        for m in range(8):
                            c = half * W + m * CH
                            ins = head64(bank, m * CH, [(lhs[:, c:c + CH], rhs[:, c:c + CH], CH, m == 0, m == 7)])
                        done(ins, kind)

            def batch(kind, l, half, lhs, rhs):
                bank = claim(kind, l, half)
                for m in range(8):
                    c = half * W + m * CH
                    rr = cc("eye") if rhs is None else rhs[:, c:c + CH]
                    ins = head64(bank, m * CH, [(lhs[:, c:c + CH], rr, CH, m == 0, m == 7)])
                done(ins, kind)

            def inv(l):
                for half in range(2):
                    pe.wait_ge(S("level_ready"), 2 * l + half + 1)
                    if l > 0:
                        drained(pe, "iZ" if l == 1 else "iX", l - 1, half)
                    batch("iT" if l else "iZ", l, half, Lm, X if l else None)
                if l == 0:
                    return
                for half in range(2):
                    drained(pe, "iT", l, half)
                    if l == 1:
                        pe.wait_ge(S("xt_ready"), 2)
                    else:
                        drained(pe, "iXT", l - 1, half)
                    if l < LEVELS - 1:
                        batch("iX", l, half, XT, Tm)
                    batch("iXT", l, half, Tm, XT)

            def pr(ap, p, n=CH):
                return ap[:, p * n:(p + 1) * n]

            def seq(c):
                bank = claim("sR", c)
                for k in ("lab", "lak", "lrb", "lrk"):
                    drained(pe, k, 1)
                for k in ("vt", "kt", "bt"):
                    drained(pe, k, 1)
                for p in range(PAIRS):
                    m = p * NCH + c
                    ins = head64(bank, p * CH, [(pr(LakT, m), pr(Vt, m), CH, p == 0, False)])
                if c == 0:
                    pe.wait_ge(S("state_zero"), 1)
                else:
                    drained(pe, "sS", c - 1)
                for p in range(PAIRS):
                    m = p * NCH + c
                    ins = head64(bank, p * CH, [(pr(at_, m), pr(stS[c % 2], p), CH, False, p == PAIRS - 1)])
                done(ins, "sR")
                bank = claim("sS", c)
                for p in range(PAIRS):
                    m = p * NCH + c
                    head64(bank, p * CH, [(pr(Kt, m), pr(Vt, m), CH, p == 0, False)])
                ubank = claim("sU", c)
                drained(pe, "iXT", LEVELS - 1, 0)
                drained(pe, "iXT", LEVELS - 1, 1)
                drained(pe, "sR", c)
                for p in range(PAIRS):
                    m = p * NCH + c
                    ins = head64(ubank, p * CH, [(pr(XT, m), pr(Rb, p), CH, p == 0, p == PAIRS - 1)])
                done(ins, "sU")
                ybank = claim("sY", c)
                for p in range(PAIRS):
                    m = p * NCH + c
                    head64(ybank, p * CH, [(pr(Vt, m), pr(LrkT, m), CH, p == 0, False),
                                           (pr(stS[c % 2], p), pr(r_, m), CH, False, False)])
                drained(pe, "sU", c)
                for p in range(PAIRS):
                    m = p * NCH + c
                    ins = head64(bank, p * CH, [(pr(Bt, m), pr(Ub, p), CH, False, p == PAIRS - 1)])
                done(ins, "sS")
                for p in range(PAIRS):
                    m = p * NCH + c
                    ins = head64(ybank, p * CH, [(pr(Ub, p), pr(LrbT, m), CH, False, p == PAIRS - 1)])
                done(ins, "sY")

            def gn(_):
                for c in range(NCH):
                    drained(pe, "sY", c)
                for half in range(2):
                    done(mm(claim("gm", half)[:, :], cc("jblk"), yB[:, half * W:(half + 1) * W], start=True, stop=True), "gm")

            def gn2(_):
                pe.wait_ge(S("gnsq_ready"), 1)
                for half in range(2):
                    done(mm(claim("gv", half)[:, :], cc("jblk"), gnq[:, half * W:(half + 1) * W], start=True, stop=True), "gv")

            def az(g):
                for kind in ("aq", "ak", "av"):
                    w = weights(pe, (kind, g))
                    for t in range(NT):
                        bank = claim(kind, g, t)
                        for kc in range(KC):
                            ins = mm(bank[:, :], hT[:, kc, t * P:(t + 1) * P], w[:, kc * W:(kc + 1) * W],
                                     start=(kc == 0), stop=(kc == KC - 1))
                        done(ins, kind)

            def attn_s(g):
                if g < NG:
                    for i, (kind, src) in enumerate((("aqT", zq), ("akT", zk))):
                        for t in range(NT):
                            pe.wait_ge(S("rot_done"), (g * 2 + i) * NT + t + 1)
                            bank = claim(kind, g, t)
                            for h in range(HEADS):
                                ins = nc.tensor.transpose(bank[:, h * P:(h + 1) * P], src[:, t, h * P:(h + 1) * P], ident)
                            done(ins, kind)
                for t in range(NT):
                    if g < NG:
                        drained(pe, "aqT", g, t)
                        drained(pe, "akT", g, t)
                    else:
                        drained(pe, "cqT", t)
                        drained(pe, "ckT", t)
                for t, part, h0, nh, nk, k0 in tile_parts(g):
                    bank = claim("sc", g, t, part)
                    for h in range(h0, h0 + nh):
                        ins = mm(bank[:, (h - h0) * nk:(h - h0 + 1) * nk], qT[:, h, t * P:(t + 1) * P], kT[:, h, k0:k0 + nk],
                                 start=True, stop=True)
                    done(ins, "sc")

            def attn_t(g):
                for t, part, h0, nh, nk, k0 in tile_parts(g):
                    pr_, _ = prob(g, t)
                    pe.wait_ge(S("probs_ready"), NT * ORDER_ATTN.index(g) + t + 1)
                    bank = claim("pT", g, t, part)
                    i = 0
                    for h in range(h0, h0 + nh):
                        for b in range(nk // P):
                            ins = nc.tensor.transpose(bank[:, i * P:(i + 1) * P], pr_[:, h, b * P:(b + 1) * P], ident)
                            i += 1
                    done(ins, "pT")
                for t in range(NT):
                    _, pt = prob(g, t)
                    parts = [p for p in tile_parts(g) if p[0] == t]
                    for p in parts:
                        drained(pe, "pT", g, t, p[1])
                    if g < NG:
                        for tt in range(NT):
                            drained(pe, "av", g, tt)
                    else:
                        for tt in range(NT):
                            drained(pe, "cv", tt)
                    nb = parts[0][4] // P
                    bank = claim("pv", g, t)
                    for h in range(HEADS):
                        for b in range(nb):
                            ins = mm(bank[:, h * P:(h + 1) * P], pt[:, h, b, :], vv[:, b, h * P:(h + 1) * P],
                                     start=(b == 0), stop=(b == nb - 1))
                    done(ins, "pv")
                if g == NG:
                    out_heads(1)

            def out_heads(n):
                for t in range(NT):
                    pe.wait_ge(S("o_ready"), NT * (n - 1) + t + 1)
                    bank = claim("oT", n, t)
                    for h in range(HEADS):
                        ins = nc.tensor.transpose(bank[:, h * P:(h + 1) * P], O[:, t, h * P:(h + 1) * P], ident)
                    done(ins, "oT")

            def gates(b):
                wb = weights(pe, ("wb", b))
                wgs = []
                for half in range(2):
                    wg = weights(pe, (f"g{half}", b))
                    wgs.append(wg)
                    for c in range(4):
                        bank = claim("gz", b, 4 * half + c)
                        done(channel_chunk(bank, wg, c, hT), "gz")
                        if half == 0 and c == 0:
                            if b == 1:
                                pe.wait_ge(S("yb_ready"), 1)
                            else:
                                for t in range(NT):
                                    drained(pe, "oT", 1 if b == 2 else 2, t)
                        bank = claim("pj", b, 4 * half + c)
                        done(channel_chunk(bank, wb, 4 * half + c, yT, nk=HEADS, width=D), "pj")

            def wo(_):
                pe.wait_ge(S("merged_ready"), (NG - 1) * KC)
                for half in range(2):
                    w = weights(pe, ("wo", half))
                    for t in range(NT):
                        bank = claim("wo", t, half)
                        for kc in range(KC):
                            ins = mm(bank[:, :], merged[:, kc, t * P:(t + 1) * P], w[:, kc * W:(kc + 1) * W],
                                     start=(kc == 0), stop=(kc == KC - 1))
                        done(ins, "wo")

            stages = {"vec": vec, "normx": lambda _: turn("hT", hx, "h_ready"), "normm": lambda _: turn("mT", memx, "memn_ready"),
                      "rz": rz, "lora": lora, "ck": ck, "cv": cv, "cq": cq, "kk": kkn, "bonus": bonus, "tok": tok, "L": L,
                      "inv": inv, "seq": seq, "gn": gn, "gn2": gn2, "az": az, "attn_s": attn_s, "attn_t": attn_t,
                      "outA": lambda _: out_heads(2), "gates": gates, "wo": wo}
            for st, arg in ORDER:
                if st in stages:
                    stages[st](arg)

            turn("nT", xn, "xn_ready")
            for t in range(NT):
                for half in range(2):
                    drained(pe, "nT", t, half)
            pe.wait_ge(S("late_landed"), 16 * 4)
            for t in range(NT):
                bank = claim("rl", t)
                for kc in range(KC):
                    ins = mm(bank[:, 0:E], hnT[:, kc, t * P:(t + 1) * P], rw[:, kc, :], start=(kc == 0), stop=(kc == KC - 1))
                done(ins, "rl")
            bank = claim("b1")
            for q in range(4):
                ins = nc.tensor.transpose(bank[:, q * P:(q + 1) * P], b1raw[:, q * P:(q + 1) * P], ident)
            done(ins, "b1")
            pe.wait_ge(S("sel_ready"), NT)
            bank = claim("rk", 0)
            done(mm(bank[:, 0:E], cc("earlier"), sel[:, 0, :], start=True, stop=True), "rk")
            bank = claim("rk", 1)
            mm(bank[:, 0:E], cc("ones"), sel[:, 0, :], start=True, stop=False)
            done(mm(bank[:, 0:E], cc("earlier"), sel[:, 1, :], start=False, stop=True), "rk")
            pe.wait_ge(S("gate_ready"), NT)
            bank = claim("wT")
            for t in range(NT):
                ins = nc.tensor.transpose(bank[0:E, t * P:(t + 1) * P], gate[:, t, 0:E], ident)
            done(ins, "wT")
            drained(pe, "wT")
            for t in range(NT):
                for half in range(2):
                    done(mm(claim("b2", t, half)[:, :], WT[:, t * P:(t + 1) * P], b2s[:, half * W:(half + 1) * W],
                            start=True, stop=True), "b2")
            for kind, idx in in_bank[-8:]:
                drained(pe, kind, *idx)

            def gather(n):
                pe.wait_ge(S("G_ready"), n + 1)
                for kc in range(KC):
                    for t in range(NT):
                        ins = mm(XG[:, kc * CAP:(kc + 1) * CAP], xn[:, t, kc * P:(kc + 1) * P], G[:, t, :],
                                 start=(t == 0), stop=(t == NT - 1))
                ins.then_inc(S("xg_filled"), 1)

            def scatter(q, t):
                if t == 0:
                    pe.wait_ge(S("y_evac"), q + 1)
                    pe.wait_ge(S("gt_evac"), q + 1)
                reached(pe, "c_added", 4 * q + 2 * t)
                for half, s in enumerate((LO, HI)):
                    mm((C0, C1)[half][:, :], GTw[s, t * P:(t + 1) * P], ysb[s, :],
                       start=True, stop=True).then_inc(S("c_filled"), 1)

            def turn_u(i):
                for b in range(4):
                    ins = nc.tensor.transpose((TU, U0)[i][:, b * P:(b + 1) * P], usb[:, i * W + b * P:i * W + (b + 1) * P], ident)
                ins.then_inc(S("tu_filled"), 1)

            def expert(k, n):
                pe.wait_ge(S("xg_evac"), n + 1)
                reached(pe, "act_ready", k)
                for i, bank in enumerate((U0, U1)):
                    pe.wait_ge(S(f"slot_landed{2 * i}"), 16 * base[2 * i] + 16 * k + 16)
                    pe.wait_ge(S(f"slot_landed{2 * i + 1}"), 16 * base[2 * i + 1] + 16 * k + 16)
                    for kc in range(KC):
                        for j, s in enumerate((LO, HI)):
                            ins = mm(bank[s, :], xgT[:, kc, :], ring[:, 2 * i + j, kc * W:(kc + 1) * W],
                                     start=(kc == 0), stop=(kc == KC - 1))
                            if kc == KC - 1:
                                ins.then_inc(S(f"slot_used{2 * i + j}"), 1)
                scatter(n, 0)
                pe.wait_ge(S("u_evac"), 2 * k + 1)
                turn_u(0)
                pe.wait_ge(S("Gw_ready"), k + 1)
                pe.wait_ge(S("gt_evac"), n + 1)
                gather(n + 1)
                for t in range(NT):
                    ins = nc.tensor.transpose(GB[:, t * P:(t + 1) * P], Gw[:, t, :], ident)
                ins.then_inc(S("gt_filled"), 1)
                pe.wait_ge(S("u_evac"), 2 * k + 2)
                turn_u(1)
                scatter(n, 1)
                pe.wait_ge(S("act_ready"), k + 1)
                for s in range(2):
                    pe.wait_ge(S(f"slot_landed{4 + s}"), 16 * k + 16)
                    for j in range(4):
                        for half, hs in enumerate((LO, HI)):
                            ins = mm(YB[hs, :], actT[:, (2 * j + s) * CAP:(2 * j + s + 1) * CAP],
                                     ring[:, 4 + s, j * D + half * W:j * D + (half + 1) * W],
                                     start=(s + j == 0), stop=(s + j == 4))
                    ins.then_inc(S(f"slot_used{4 + s}"), 1)

            def serve(r):
                pe.wait_ge(S("xg_evac"), r * (E + 1))
                gather(r * (E + 1))
                expert(r * E, r * (E + 1))
                with pe.Fori(1, E) as e:
                    expert(r * E + e, r * (E + 1) + e)
                scatter(r * (E + 1) + E, 0)
                scatter(r * (E + 1) + E, 1)

            serve(0)
            pe.wait_ge(S("flag_ready"), 1)
            more = pe.value_load(flagi[0:1, 0:1], min_val=0, max_val=1)
            with pe.If(more > 0):
                with pe.Fori(1, T // CAP) as r:
                    serve(r)

        @block.vector
        def _(dve):
            v = nc.vector
            steps = [0]

            def link(ins):
                steps[0] += 1
                ins.then_inc(S("dve_step"), 1)
                dve.wait_ge(S("dve_step"), steps[0])

            def drain(ins, kind):
                ins.then_inc(Drained(kind), 1)

            tt, ts, stt = v.tensor_tensor, v.tensor_scalar, v.scalar_tensor_tensor

            def vec(_):
                ps = filled(dve, "vec")
                drain(v.tensor_copy(vecT[:, :], ps[:, 0:NROWS]), "vec")
                drained(dve, "vec")
                link(ts(omm[:, :], vcol("r_mu", 0, 14), -1.0, 1.0, ALU.mult, ALU.add))
                ts(omka[:, :], vcol("r_k_a", 0, 4), -1.0, 1.0, ALU.mult, ALU.add).then_inc(S("omm_ready"), 1)

            def angle(_):
                dve.wait_ge(S("pos_landed"), 16)
                dve.wait_ge(S("const_landed"), 16)
                link(v.tensor_copy(posf[:, :], posi[:, :]))
                ang = A1[:, 5, 0:NT * HALF].rearrange("p (t k) -> p t k", t=NT)
                kf = A1[:, 5, 64:64 + NT * HALF].rearrange("p (t k) -> p t k", t=NT)
                rs = A1[:, 5, 128:128 + NT * HALF].rearrange("p (t k) -> p t k", t=NT)
                rc = A1[:, 5, 192:192 + NT * HALF].rearrange("p (t k) -> p t k", t=NT)
                link(tt(ang, rep(cc("invf"), NT), each(posf[:, :], HALF), ALU.mult))
                magic = 1.5 * 2.0 ** 23
                link(ts(kf, ang, 1.0 / (2 * math.pi), None, ALU.mult))
                link(ts(kf, kf, magic, None, ALU.add))
                link(ts(kf, kf, -magic, None, ALU.add))
                rest, pieces = 2 * math.pi, []
                for bits in (5, 13, 22):
                    piece = math.floor(rest * 2.0 ** bits) / 2.0 ** bits
                    pieces.append(piece)
                    rest -= piece
                pieces.append(rest)
                for i, piece in enumerate(pieces):
                    link(stt(rs, kf, -piece, ang if i == 0 else rs, ALU.mult, ALU.add))
                link(ts(rc, rs, math.pi / 2, None, ALU.add))
                link(ts(kf, rc, math.pi, -2 * math.pi, ALU.is_gt, ALU.mult))
                link(tt(rc, rc, kf, ALU.add))
                lim = 3.1415925
                ts(rs, rs, lim, -lim, ALU.min, ALU.max)
                ts(rc, rc, lim, -lim, ALU.min, ALU.max).then_inc(S("angle_ready"), 1)

            def scaled(name, src, dst, sem, i):
                dve.wait_ge(S("rstd_ready"), NORMS.index(name) + 1)
                for t in range(NT):
                    ts(dst[:, t, :], src[:, t, :], rst[:, i + t:i + t + 1], None, ALU.mult).then_inc(S(sem), 1)

            def turned(kind, gain, dst):
                for t in range(NT):
                    for half in range(2):
                        ps = filled(dve, kind, t, half)
                        drain(tt(dst[:, 4 * half:4 * half + 4, t * P:(t + 1) * P],
                                 ps[:, :].rearrange("p (a b) -> p a b", b=P),
                                 each(vcol(gain, 4 * half, 4), P), ALU.mult), kind)

            def normx(_):
                scaled("x", x, hx, "h_ready", 0)
                turned("hT", "norm_mix", hT)

            def normm(_):
                scaled("mem", memx, memx, "memn_ready", 2)
                turned("mT", "mem_norm", memT)

            dst_rz = [ch(r_), ch(k_), ch(v_), wag]

            def rz(i):
                for c in range(4 if i < 3 else 2):
                    n = 4 * i + c
                    ps = filled(dve, "rz", n)
                    dve.wait_ge(S("rz_scaled"), n + 1)
                    d = dst_rz[i][:, c, 1:T]
                    drain(stt(d, ps[:, 0:T - 1], vcol("r_mu", n), d, ALU.mult, ALU.add), "rz")

            def kkn(_):
                for p in range(PAIRS):
                    ins = ts(ch(kk)[:, p, :], ch(k_)[:, p, :], vcol("r_k_k", p), None, ALU.mult)
                    if p % 2:
                        ins.then_inc(S("kk_raw"), 1)
                drained(dve, "la", PAIRS - 1)
                for p in range(PAIRS):
                    ins = v.tensor_tensor_scan(ch(cum)[:, p, :], cc("reset"), ch(sgw)[:, p, :], 0.0, ALU.mult, ALU.add)
                ins.then_inc(S("cum_ready"), 1)
                for half in range(2):
                    drained(dve, "kn", half)
                    s = slice(half * W, (half + 1) * W)
                    link(ts(tmp7[:, s], tmp7[:, s], 1e-12, None, ALU.max))
                    link(v.reciprocal(tmp7[:, s], tmp7[:, s]))
                    link(tt(kk[:, s], kk[:, s], tmp7[:, s], ALU.mult))
                for p in range(PAIRS):
                    ins = ts(ch(tmp7)[:, p, :], ch(a_)[:, p, :], vcol("r_k_a", p), omka[:, p:p + 1], ALU.mult, ALU.add)
                link(ins)
                link(tt(k_, k_, tmp7, ALU.mult))
                for p in range(PAIRS):
                    ins = stt(ch(tmp6)[:, p, :], ch(r_)[:, p, :], vcol("r_r_k", p), ch(k_)[:, p, :], ALU.mult, ALU.mult)
                ins.then_inc(S("rkk_ready"), 1)

            def bonus(_):
                for half in range(2):
                    ps = filled(dve, "bn", half)
                    s = slice(half * W, (half + 1) * W)
                    drain(tt(bv[:, s], ps[:, :], v_[:, s], ALU.mult), "bn")

            def tilde(_):
                dve.wait_ge(S("exps_ready"), 3)
                dve.wait_ge(S("ept_ready"), 1)
                stt(at_, kk, -1.0, sgw, ALU.mult, ALU.mult)
                link(tt(bt_, kk, a_, ALU.mult))
                tt(bt_, bt_, eN, ALU.mult)
                tt(k_, k_, eN, ALU.mult)
                tt(r_, r_, cum, ALU.mult).then_inc(S("tilde_ready"), 1)

            def head_norm(kind, idx, name, gain, col, dst):
                t = idx[-1]
                ps = filled(dve, kind, *idx)
                dve.wait_ge(S("rstd_ready"), NORMS.index(name) + 1)
                for h in range(HEADS):
                    ins = stt(dst[:, t, h * HD:(h + 1) * HD], ps[:, h * HD:(h + 1) * HD],
                              rst[:, col + h:col + h + 1], gains[:, gain, :], ALU.mult, ALU.mult)
                drain(ins, kind)

            def ck(_):
                dve.wait_ge(S("gains_landed"), 64)
                for t in range(NT):
                    head_norm("ck", (t,), ("ck", t), 3, 8 + 4 * t, zk)

            def cq(_):
                for t in range(NT):
                    head_norm("cq", (t,), ("cq", t), 2, 16 + 4 * t, zq)

            def az(g):
                for i, (kind, dst) in enumerate((("aq", zq), ("ak", zk))):
                    for t in range(NT):
                        head_norm(kind, (g, t), ("qk"[i:i + 1], g, t), i, 24 + 16 * g + 8 * i + 4 * t, dst)

            def attn_s(g):
                m_new, m_old = mx[:, g % 2, :, :], mx[:, (g + 1) % 2, :, :]
                n_at = ORDER_ATTN.index(g)
                for t in range(NT):
                    pr_, _ = prob(g, t)
                    parts = [p for p in tile_parts(g) if p[0] == t]
                    for _t, part, h0, nh, nk, k0 in parts:
                        ps = filled(dve, "sc", g, t, part)
                        s3 = ps[:, 0:nh * nk].rearrange("p (h k) -> p h k", k=nk)
                        if g < NG:
                            a = CONST["amask"][0] + 256 * g + (128 if t == 0 else 0)
                            drain(stt(pr_[:, h0:h0 + nh, :], s3, SCALE, rep(const[:, a:a + nk], nh), ALU.mult, ALU.add), "sc")
                        else:
                            drain(ts(pr_[:, h0:h0 + nh, :], s3, SCALE, None, ALU.mult), "sc")
                        drained(dve, "sc", g, t, part)
                    if g in (0, NG):
                        link(v.tensor_reduce(m_new[:, t, :], pr_, AX, ALU.max))
                    else:
                        link(v.tensor_reduce(mx[:, 3, t, :], pr_, AX, ALU.max))
                        link(tt(m_new[:, t, :], mx[:, 3, t, :], m_old[:, t, :], ALU.max))
                        link(tt(mx[:, 4, t, :], m_old[:, t, :], m_new[:, t, :], ALU.subtract))
                    ts(mx[:, 2, t, :], m_new[:, t, :], -1.0, None, ALU.mult).then_inc(S("max_ready"), 1)

            def attn_t(g):
                n_at = ORDER_ATTN.index(g)
                for t in range(NT):
                    ps = filled(dve, "pv", g, t)
                    dve.wait_ge(S("probs_ready"), NT * n_at + t + 1)
                    if g in (0, NG):
                        if g == 0 and t == 0:
                            for tt_ in range(NT):
                                dve.wait_ge(S("oT_filled"), ledger[("oT", (1, tt_))][1])
                        drain(v.tensor_copy(O[:, t, :], ps[:, :]), "pv")
                        link(v.tensor_copy(lsum[:, 0, t, :], lsum[:, 1, t, :]))
                    else:
                        o3 = O[:, t, :].rearrange("p (h k) -> p h k", k=HD)
                        tt(lsum[:, 0, t, :], lsum[:, 0, t, :], mx[:, 5, t, :], ALU.mult)
                        link(tt(o3, o3, each(mx[:, 5, t, :], HD), ALU.mult))
                        tt(lsum[:, 0, t, :], lsum[:, 0, t, :], lsum[:, 1, t, :], ALU.add)
                        drain(tt(O[:, t, :], O[:, t, :], ps[:, :], ALU.add), "pv")
                    drained(dve, "pv", g, t)
                    if g in (NG, NG - 1):
                        link(v.reciprocal(mx[:, 3, t, :], lsum[:, 0, t, :]))
                        o3 = O[:, t, :].rearrange("p (h k) -> p h k", k=HD)
                        tt(o3, o3, each(mx[:, 3, t, :], HD), ALU.mult).then_inc(S("o_ready"), 1)

            def gates(b):
                n0 = ORDER_GATES.index(b) * KC
                for c in range(KC):
                    ps = filled(dve, "pj", b, c)
                    drained(dve, "gz", b, c)
                    if ORDER_GATES.index(b) == 0:
                        tt(merged[:, c, :], ps[:, 0:T], sg[c % 2], ALU.mult).then_inc(S("pj_drained"), 1)
                    else:
                        tt(gp[c % 2], ps[:, 0:T], sg[c % 2], ALU.mult).then_inc(S("pj_drained"), 1)
                        dve.wait_ge(S("pj_drained"), ledger[("pj", (b, c))][1])
                        tt(merged[:, c, :], merged[:, c, :], gp[c % 2], ALU.add).then_inc(S("merged_ready"), 1)

            def L(_):
                for kind, dst, mask in (("lab", LabT, "strict"), ("lak", LakT, "strict"), ("lrb", LrbT, "incl"), ("lrk", LrkT, "incl")):
                    for half in range(2):
                        ps = filled(dve, kind, half)
                        s = slice(half * W, (half + 1) * W)
                        drain(tt(mm64(dst[:, s]), mm64(ps[:, :]), rep(cc(mask), 8), ALU.mult), kind)

            def inv(l):
                if l == 0:
                    for half in range(2):
                        s = slice(half * W, (half + 1) * W)
                        dve.wait_ge(S("level_ready"), half + 1)
                        filled(dve, "lrk", 1)
                        tt(mm64(XT[:, s]), mm64(Lm[:, s]), rep(cc("eye"), 8), ALU.add).then_inc(S("xt_ready"), 1)
                        ps = filled(dve, "iZ", 0, half)
                        drain(tt(mm64(X[:, s]), mm64(ps[:, :]), rep(cc("eye"), 8), ALU.add), "iZ")
                    return
                for half in range(2):
                    s = slice(half * W, (half + 1) * W)
                    if l < LEVELS - 1:
                        ps = filled(dve, "iX", l, half)
                        drain(tt(X[:, s], X[:, s], ps[:, :], ALU.add), "iX")
                    ps = filled(dve, "iXT", l, half)
                    drain(tt(XT[:, s], XT[:, s], ps[:, :], ALU.add), "iXT")

            def seq(c):
                ps = filled(dve, "sR", c)
                if c == 0:
                    dve.wait_ge(S("iT_filled"), ledger[("iT", (LEVELS - 1, 1))][1])
                drain(v.tensor_copy(Rb, ps[:, 0:256]), "sR")
                ps = filled(dve, "sU", c)
                drain(v.tensor_copy(Ub, ps[:, 0:256]), "sU")
                ps = filled(dve, "sS", c)
                new = stS[(c + 1) % 2]
                if c == 0:
                    dve.wait_ge(S("state_zero"), 1)
                link(tt(new, stS[c % 2], ps[:, 0:256], ALU.add))
                drain(tt(mm64(new), mm64(new), each(ePT[:, :, c], CH), ALU.mult), "sS")
                ps = filled(dve, "sY", c)
                drain(v.tensor_copy(ch(yB)[:, :, c * CH:(c + 1) * CH], mm64(ps[:, 0:256])), "sY")

            def gn(_):
                for half in range(2):
                    ps = filled(dve, "gm", half)
                    s = slice(half * W, (half + 1) * W)
                    drain(stt(gnd[:, s], ps[:, :], -1.0 / RD, yB[:, s], ALU.mult, ALU.add), "gm")
                drained(dve, "gm", 1)
                tt(gnq, gnd, gnd, ALU.mult).then_inc(S("gnsq_ready"), 1)

            def gn2(_):
                for half in range(2):
                    ps = filled(dve, "gv", half)
                    s = slice(half * W, (half + 1) * W)
                    drain(ts(gnr[:, s], ps[:, :], 1.0 / RD, GN_EPS, ALU.mult, ALU.add), "gv")
                dve.wait_ge(S("gn_root"), 1)
                link(v.reciprocal(gnr, gnr))
                link(tt(gnd, gnd, gnr, ALU.mult))
                for p in range(PAIRS):
                    ins = ts(ch(gnd)[:, p, :], ch(gnd)[:, p, :], vcol("r_ln_w", p), vcol("r_ln_b", p), ALU.mult, ALU.add)
                link(ins)
                link(tt(gnd, gnd, bv, ALU.add))
                dve.wait_ge(S("pj_filled"), ledger[("pj", (2, KC - 1))][1])
                tt(yT[:, :, :].rearrange("p a b -> p (a b)"), gnd, g_, ALU.mult).then_inc(S("yb_ready"), 1)

            def wo(_):
                for half in range(2):
                    for t in range(NT):
                        ps = filled(dve, "wo", t, half)
                        s = slice(half * W, (half + 1) * W)
                        drain(tt(x[:, t, s], x[:, t, s], ps[:, :], ALU.add), "wo")

            stages = {"vec": vec, "normx": normx, "angle": angle, "normm": normm, "rz": rz, "kk": kkn, "bonus": bonus, "tilde": tilde,
                      "ck": ck, "cq": cq, "az": az, "attn_s": attn_s, "attn_t": attn_t, "gates": gates, "L": L, "inv": inv,
                      "seq": seq, "gn": gn, "gn2": gn2, "wo": wo}
            for st, arg in ORDER:
                if st in stages:
                    stages[st](arg)

            drained(dve, "wo", 1, 1)
            scaled("ffn", x, xn, "xn_ready", 4)
            turned("nT", "norm_ffn", hnT)
            dve.wait_ge(S("late_landed"), 16 * 4)
            dve.wait_ge(S("zero_ready"), 1)
            for t in range(NT):
                ps = filled(dve, "rl", t)
                top, g8 = small[:, t, :], flag
                drain(tt(lgt[:, t, :], ps[:, 0:E], rbias, ALU.add), "rl")
                drained(dve, "rl", t)
                link(v.max(top, lgt[:, t, :]))
                link(ts(sel[:, t, :], lgt[:, t, :], top[:, 3:4], None, ALU.is_gt))
                ts(eqs[:, t, :], lgt[:, t, :], top[:, 3:4], None, ALU.is_equal)
                link(v.tensor_reduce(flag[:, t:t + 1], sel[:, t, :], AX, ALU.add))
                ts(flag[:, 2 + t:3 + t], flag[:, t:t + 1], -1.0, float(TOPK), ALU.mult, ALU.add)
                link(v.tensor_tensor_scan(cnt[:, t, :], eqs[:, t, :], zer, 0.0, ALU.add, ALU.add))
                link(ts(tie[:, t, :], cnt[:, t, :], flag[:, 2 + t:3 + t], None, ALU.is_le))
                link(tt(tie[:, t, :], tie[:, t, :], eqs[:, t, :], ALU.mult))
                tt(sel[:, t, :], sel[:, t, :], tie[:, t, :], ALU.add).then_inc(S("sel_ready"), 1)
                ts(top[:, 7:8], top[:, 0:1], -1.0, None, ALU.mult).then_inc(S("top_ready"), 1)
            for t in range(NT):
                dve.wait_ge(S("lexp_ready"), t + 1)
                link(tt(gate[:, t, 0:E], eqs[:, t, :], sel[:, t, :], ALU.mult))
                link(v.tensor_reduce(flag[:, t:t + 1], gate[:, t, 0:E], AX, ALU.add))
                link(v.reciprocal(flag[:, t:t + 1], flag[:, t:t + 1]))
                ts(gate[:, t, 0:E], gate[:, t, 0:E], flag[:, t:t + 1], None, ALU.mult).then_inc(S("gate_ready"), 1)
            for t in range(NT):
                ps = filled(dve, "rk", t)
                drain(stt(rank[:, t, 0:E], ps[:, 0:E], UNSEL, sel[:, t, :], ALU.add, ALU.mult), "rk")
                drained(dve, "rk", t)
                link(ts(rank[:, t, 0:E], rank[:, t, 0:E], -UNSEL, None, ALU.add))
            v.tensor_reduce(flag[:, 3:4], EA[:, 2, 256:256 + 2 * (E + 1)], AX, ALU.max).then_inc(S("rmax_ready"), 1)
            ps = filled(dve, "b1")
            drain(v.tensor_copy(b1T, ps[:, :]), "b1")
            for t in range(NT):
                for half in range(2):
                    ps = filled(dve, "b2", t, half)
                    s = slice(half * W, (half + 1) * W)
                    drain(tt(x[:, t, s], x[:, t, s], ps[:, :], ALU.add), "b2")
            dve.wait_ge(S("allmax_ready"), 1)
            link(ts(flag[:, 1:2], flag[:, 0:1], float(CAP) - 0.5, None, ALU.is_gt))
            v.tensor_copy(flagi[:, :], flag[:, 1:2]).then_inc(S("flag_ready"), 1)

            def one_hot(e):
                for t in range(NT):
                    ins = ts(G[:, t, :], cc("iota"), rank[:, t, bass.ds(e, 1)], None, ALU.is_equal)
                ins.then_inc(S("G_ready"), 1)

            def gathered(n):
                dve.wait_ge(S("xg_filled"), n + 1)
                tt(xgT, XG[:, :].rearrange("p (k c) -> p k c", c=CAP), each(vcol("norm_ffn", 0, KC), CAP),
                   ALU.mult).then_inc(S("xg_evac"), 1)

            def add_back(q, t):
                for half in range(2):
                    s = slice(half * W, (half + 1) * W)
                    dve.wait_ge(S("c_filled"), 4 * q + 2 * t + half + 1)
                    tt(x[:, t, s], x[:, t, s], (C0, C1)[half][:, :], ALU.add).then_inc(S("c_added"), 1)

            def expert(e, k, n, sem, cnt_):
                def own(ins, i):
                    ins.then_inc(S(sem), 1)
                    dve.wait_ge(S(sem), cnt_ + i)

                reached(dve, "gt_filled", k)
                for t in range(NT):
                    ins = ts(Gw[:, t, :].rearrange("p (h c) -> p h c", h=2), rep(cc("iota"), 2), rank[:, t, bass.ds(e, 1)], gate[:, t, bass.ds(e, 1)],
                             ALU.is_equal, ALU.mult)
                ins.then_inc(S("Gw_ready"), 1)
                dve.wait_ge(S("xg_filled"), n + 1)
                one_hot(e + 1)
                add_back(n, 0)

                def biased(dst, bank, i):
                    bias = b1T[:, bass.ds(e * 16 + 8 * i, 8)].rearrange("p (h b) -> p b h", b=4)
                    return tt(dst.rearrange("p (b h c) -> p b h c", h=2, c=CAP),
                              bank[:, :].rearrange("p (b h c) -> p b h c", h=2, c=CAP),
                              bias.unsqueeze(3).to_broadcast([P, 4, 2, CAP]), ALU.add)

                dve.wait_ge(S("tu_filled"), 2 * k + 1)
                own(biased(glu, TU, 0), 1)
                ts(glu, glu, LIMIT, None, ALU.min).then_inc(S("glu_ready"), 1)
                dve.wait_ge(S("tu_filled"), 2 * k + 2)
                own(biased(lin, U0, 1), 2)
                own(ts(lin, lin, LIMIT, -LIMIT, ALU.min, ALU.max), 3)
                own(stt(lin, lin, 1.0, glu, ALU.add, ALU.mult), 4)
                dve.wait_ge(S("sig_ready"), k + 1)
                reached(dve, "slot_used5", k)
                tt(actT, lin, sig, ALU.mult).then_inc(S("act_ready"), 1)
                gathered(n + 1)
                add_back(n, 1)

            def serve(r):
                if not isinstance(r, int):
                    dve.wait_ge(S("Gw_ready"), r * E)
                    ts(EA[:, 2, 256:256 + 2 * (E + 1)], EA[:, 2, 256:256 + 2 * (E + 1)], -float(CAP), None,
                       ALU.add).then_inc(S("rank_shifted"), 1)
                    dve.wait_ge(S("rank_shifted"), r)
                v.memset(ysb, 0.0).then_inc(S("y_evac"), 1)
                v.memset(GTw, 0.0).then_inc(S("gt_evac"), 1)
                reached(dve, "xg_filled", r * (E + 1))
                one_hot(0)
                gathered(r * (E + 1))
                expert(0, r * E, r * (E + 1), "expert_step", 4 * r * E)
                with dve.Fori(1, E) as e:
                    expert(e, r * E + e, r * (E + 1) + e, "expert_step", 4 * (r * E + e))
                for t in range(NT):
                    add_back(r * (E + 1) + E, t)

            serve(0)
            dve.wait_ge(S("flag_ready"), 1)
            more = dve.value_load(flagi[0:1, 0:1], min_val=0, max_val=1)
            with dve.If(more > 0):
                with dve.Fori(1, T // CAP) as r:
                    serve(r)
            v.engine_nop().then_inc(S("all_added"), 1)

        @block.scalar
        def _(act):
            a = nc.scalar

            def drain(ins, kind):
                ins.then_inc(Drained(kind), 1)

            def copy(o, i):
                return a.activation(o, i, ACT.Copy)

            act.dma_start(ident, A["consts"][:, 0:P]).then_inc(S("ident_landed"), 16)
            for name in list(ROWS)[0::2]:
                act.dma_start(row_tile(name), row_source(name)).then_inc(S("rows_landed"), 16)
            act.dma_start(posi[:, :], A["positions"].rearrange("o (t p) -> p (o t)", p=P), allow_slow_non_contiguous=True).then_inc(S("pos_landed"), 16)
            act.dma_start(const[:, P:NCONST], A["consts"][:, P:NCONST]).then_inc(S("const_landed"), 16)
            for i, name in enumerate(("a_q_gain", "a_k_gain", "c_q_gain", "c_k_gain")):
                act.dma_start(gains[:, i, :], A[name].to_broadcast([P, HD])).then_inc(S("gains_landed"), 16)
            act.dma_start(w2a[0:64, :], A["r_w2"][0]).then_inc(S("lora_landed"), 16)
            act.dma_start(w2a[64:128, :], A["r_a2"][0]).then_inc(S("lora_landed"), 16)
            act.dma_start(g2w, A["r_g2"][0]).then_inc(S("lora_landed"), 16)

            def squares(name, i, n, src, junk, wait=True):
                if NORMS.index(name):
                    act.wait_ge(S("squares_ready"), NORMS.index(name))
                for j in range(n):
                    ins = a.activation(junk(j), src(j), ACT.Square, accum_out=ssq[:, i + j:i + j + 1])
                ins.then_inc(S("squares_ready"), 1)

            def vec(_):
                pass

            def normx(_):
                act.wait_ge(S("x_landed"), 16)
                squares("x", 0, NT, lambda t: x[:, t, :], lambda t: A1[:, 3 + t, :])

            def angle(_):
                act.wait_ge(S("mem_landed"), 16)
                squares("mem", 2, NT, lambda t: memx[:, t, :], lambda t: A1[:, 3 + t, :])
                act.wait_ge(S("angle_ready"), 1)
                rs = A1[:, 5, 128:128 + NT * HALF].rearrange("p (t k) -> p t k", t=NT)
                rc = A1[:, 5, 192:192 + NT * HALF].rearrange("p (t k) -> p t k", t=NT)
                a.activation(trig[:, :, 0:HALF], rc, ACT.Sin)
                a.activation(trig[:, :, HALF:ROT], rc, ACT.Sin)
                a.activation(trig[:, :, ROT:ROT + HALF], rs, ACT.Sin, scale=-1.0)
                a.activation(trig[:, :, ROT + HALF:2 * ROT], rs, ACT.Sin).then_inc(S("trig_ready"), 1)

            dst_rz = [ch(r_), ch(k_), ch(v_), wag]

            def rz(i):
                if i == 0:
                    act.wait_ge(S("omm_ready"), 1)
                for c in range(4 if i < 3 else 2):
                    n = 4 * i + c
                    ps = filled(act, "rz", n)
                    a.activation(dst_rz[i][:, c, :], ps[:, 0:T], ACT.Copy, scale=omm[:, n:n + 1]).then_inc(S("rz_scaled"), 1)

            def lora(_):
                drained(act, "rz", 13)
                a.activation(wag[0:64, 0, :], wag[0:64, 0, :], ACT.Tanh).then_inc(S("wlo_ready"), 1)
                a.activation(wag[:, 1, :], wag[:, 1, :], ACT.Sigmoid).then_inc(S("wlo_ready"), 1)
                for p in range(PAIRS):
                    ps = filled(act, "lw", p)
                    drain(a.activation(ch(sgw)[:, p, :], ps[:, 0:T], ACT.Sigmoid, bias=vcol("r_w0", p)), "lw")
                    ps = filled(act, "la", p)
                    drain(a.activation(ch(a_)[:, p, :], ps[:, 0:T], ACT.Sigmoid, bias=vcol("r_a0", p)), "la")
                    ps = filled(act, "lg", p)
                    drain(copy(ch(g_)[:, p, :], ps[:, 0:T]), "lg")

            def head_squares(kind, idx, name, col):
                ps = filled(act, kind, *idx)
                squares(name, col, HEADS, lambda h: ps[:, h * HD:(h + 1) * HD], lambda h: ajunk[:, h * HD:(h + 1) * HD])

            def ck(_):
                for t in range(NT):
                    head_squares("ck", (t,), ("ck", t), 8 + 4 * t)

            def kkn(_):
                for half in range(2):
                    ps = filled(act, "kn", half)
                    drain(a.activation(tmp7[:, half * W:(half + 1) * W], ps[:, :], ACT.Sqrt), "kn")

            def cv(_):
                for t in range(NT):
                    ps = filled(act, "cv", t)
                    drain(copy(vv[:, t, :], ps[:, :]), "cv")

            def evac_T(kind, idx, dst):
                t = idx[-1]
                ps = filled(act, kind, *idx)
                drain(copy(dst[:, :, t * P:(t + 1) * P], ps[:, :].rearrange("p (h k) -> p h k", k=P)), kind)

            def cq(_):
                for t in range(NT):
                    head_squares("cq", (t,), ("cq", t), 16 + 4 * t)
                for t in range(NT):
                    evac_T("ckT", (t,), kT)
                for t in range(NT):
                    evac_T("cqT", (t,), qT)

            def tilde(_):
                act.wait_ge(S("pml_ready"), 1)
                act.wait_ge(S("cum_ready"), 1)
                a.activation(sgw, sgw, ACT.Exp, scale=LOGC).then_inc(S("exps_ready"), 1)
                a.activation(eN, cum, ACT.Exp, scale=-LOGC).then_inc(S("exps_ready"), 1)
                act.wait_ge(S("exps_ready"), 2)
                a.activation(cum, cum, ACT.Exp, scale=LOGC).then_inc(S("exps_ready"), 1)

            def attn_s(g):
                n_at = ORDER_ATTN.index(g)
                if g < NG:
                    for kind, dst in (("aqT", qT), ("akT", kT)):
                        for t in range(NT):
                            evac_T(kind, (g, t), dst)
                for t in range(NT):
                    pr_, _ = prob(g, t)
                    act.wait_ge(S("max_ready"), NT * n_at + t + 1)
                    if g not in (0, NG):
                        a.activation(mx[:, 5, t, :], mx[:, 4, t, :], ACT.Exp)
                    for h in range(HEADS):
                        ins = a.activation(pr_[:, h, :], pr_[:, h, :], ACT.Exp, bias=mx[:, 2, t, h:h + 1],
                                           accum_out=lsum[:, 1, t, h:h + 1])
                    ins.then_inc(S("probs_ready"), 1)

            def attn_t(g):
                for t, part, h0, nh, nk, k0 in tile_parts(g):
                    _, pt = prob(g, t)
                    ps = filled(act, "pT", g, t, part)
                    drain(copy(pt[:, h0:h0 + nh, :, :].rearrange("p h b k -> p (h b k)"), ps[:, 0:nh * nk]), "pT")
                if g == NG:
                    outs(1)

            def outs(n):
                for t in range(NT):
                    ps = filled(act, "oT", n, t)
                    if n == 2:
                        act.wait_ge(S("pj_filled"), ledger[("pj", (1, KC - 1))][1])
                    drain(copy(yT[:, :, t * P:(t + 1) * P], ps[:, :].rearrange("p (h k) -> p h k", k=P)), "oT")

            def gates(b):
                n0 = ORDER_GATES.index(b) * KC
                for c in range(KC):
                    ps = filled(act, "gz", b, c)
                    if c >= 2 or n0:
                        act.wait_ge(S("pj_drained"), n0 + c - 1)
                    drain(a.activation(sg[c % 2], ps[:, 0:T], ACT.Sigmoid, bias=vcol("b_gate", 8 * b + c)), "gz")

            def tok(_):
                for kind, dst in (("vt", Vt), ("kt", Kt), ("bt", Bt)):
                    for half in range(2):
                        ps = filled(act, kind, half)
                        drain(copy(dst[:, half * W:(half + 1) * W], ps[:, :]), kind)

            def az(g):
                for i, kind in enumerate(("aq", "ak")):
                    for t in range(NT):
                        head_squares(kind, (g, t), ("qk"[i:i + 1], g, t), 24 + 16 * g + 8 * i + 4 * t)
                for t in range(NT):
                    ps = filled(act, "av", g, t)
                    drain(copy(vv[:, t, :], ps[:, :]), "av")

            def inv(l):
                if l:
                    for half in range(2):
                        ps = filled(act, "iT", l, half)
                        drain(copy(Tm[:, half * W:(half + 1) * W], ps[:, :]), "iT")

            def gn2(_):
                drained(act, "gv", 1)
                a.activation(gnr, gnr, ACT.Sqrt).then_inc(S("gn_root"), 1)

            stages = {"vec": vec, "normx": normx, "angle": angle, "rz": rz, "lora": lora, "kk": kkn, "ck": ck, "cv": cv, "cq": cq,
                      "tilde": tilde, "attn_s": attn_s, "attn_t": attn_t, "outA": lambda _: outs(2), "gates": gates,
                      "tok": tok, "az": az, "inv": inv, "gn2": gn2}
            for st, arg in ORDER:
                if st in stages:
                    stages[st](arg)
            drained(act, "wo", 1, 1)
            squares("ffn", 4, NT, lambda t: x[:, t, :], lambda t: A1[:, 3 + t, :])
            for t in range(NT):
                act.wait_ge(S("top_ready"), t + 1)
                a.activation(eqs[:, t, :], lgt[:, t, :], ACT.Exp, bias=small[:, t, 7:8]).then_inc(S("lexp_ready"), 1)
            ps = filled(act, "wT")
            drain(copy(WT, ps[0:E, 0:T]), "wT")

            def expert(k, n):
                for i, bank in enumerate((U0, U1)):
                    act.wait_ge(S(f"slot_used{2 * i + 1}"), k + 1)
                    reached(act, "tu_filled", 2 * k)
                    copy(usb[:, i * W:(i + 1) * W], bank[:, :]).then_inc(S("u_evac"), 1)
                act.wait_ge(S("glu_ready"), k + 1)
                a.activation(sig, glu, ACT.Sigmoid, scale=ALPHA).then_inc(S("sig_ready"), 1)
                act.wait_ge(S("gt_filled"), k + 1)
                act.wait_ge(S("c_filled"), 4 * n + 4)
                copy(GTw, GB[:, 0:T]).then_inc(S("gt_evac"), 1)
                act.wait_ge(S("slot_used5"), k + 1)
                copy(ysb, YB[:, :]).then_inc(S("y_evac"), 1)

            def serve(r):
                expert(r * E, r * (E + 1))
                with act.Fori(1, E) as e:
                    expert(r * E + e, r * (E + 1) + e)

            serve(0)
            act.wait_ge(S("flag_ready"), 1)
            more = act.value_load(flagi[0:1, 0:1], min_val=0, max_val=1)
            with act.If(more > 0):
                with act.Fori(1, T // CAP) as r:
                    serve(r)

        @block.gpsimd
        def _(pool):
            g = nc.gpsimd
            g.memset(negh[:, :], -0.5).then_inc(S("pool_const"), 1)
            pool.wait_ge(S("pool_const"), 1)
            norm_no = [0]

            def root(col, n, width):
                norm_no[0] += 1
                i = norm_no[0]
                pool.wait_ge(S("squares_ready"), i)
                g.tensor_scalar(ssq[:, col:col + n], ssq[:, col:col + n], 1.0 / width, EPS, ALU.mult, ALU.add).then_inc(S("mean_ready"), 1)
                pool.wait_ge(S("mean_ready"), i)
                g.tensor_tensor(rst[:, col:col + n], ssq[:, col:col + n], negh[:, 0:n], ALU.pow).then_inc(S("rstd_ready"), 1)

            def normx(_):
                root(0, NT, D)

            def angle(_):
                root(2, NT, D)

            def ck(_):
                for t in range(NT):
                    root(8 + 4 * t, HEADS, HD)

            def cq(_):
                for t in range(NT):
                    root(16 + 4 * t, HEADS, HD)

            def kkn(_):
                for half in range(2):
                    s = slice(half * W, (half + 1) * W)
                    pool.wait_ge(S("kk_raw"), half + 1)
                    g.tensor_tensor(tmp6[:, s], kk[:, s], kk[:, s], ALU.mult).then_inc(S("kksq_ready"), 1)
                pool.wait_ge(S("cum_ready"), 1)
                g.tensor_tensor(sgw, cum, sgw, ALU.subtract).then_inc(S("pml_ready"), 1)

            def tilde(_):
                pool.wait_ge(S("exps_ready"), 3)
                g.tensor_copy(ePT[:, :, :], cum.rearrange("p (a c t) -> p a c t", c=NCH, t=CH)[:, :, :, CH - 1]).then_inc(S("ept_ready"), 1)

            def rotate(z, t):
                rot_no[0] += 1
                n = rot_no[0]
                z3 = z[:, t, :].rearrange("p (h k) -> p h k", k=HD)
                cos, sin = trig[:, t, 0:ROT], trig[:, t, ROT:2 * ROT]
                b0, b1 = rotb[:, 0, :, :], rotb[:, 1, :, :]
                if n > 1:
                    pool.wait_ge(S("rot_done"), n - 1)
                g.tensor_tensor(b0, z3[:, :, 0:ROT], rep(cos, HEADS), ALU.mult)
                g.tensor_tensor(b1[:, :, 0:HALF], z3[:, :, HALF:ROT], rep(sin[:, 0:HALF], HEADS), ALU.mult)
                g.tensor_tensor(b1[:, :, HALF:ROT], z3[:, :, 0:HALF], rep(sin[:, HALF:ROT], HEADS), ALU.mult).then_inc(S("rot_parts"), 1)
                pool.wait_ge(S("rot_parts"), n)
                g.tensor_tensor(z3[:, :, 0:ROT], b0, b1, ALU.add).then_inc(S("rot_done"), 1)

            rot_no = [0]

            def az(gr):
                if gr == 0:
                    pool.wait_ge(S("trig_ready"), 1)
                for i, (kind, z) in enumerate((("aq", zq), ("ak", zk))):
                    for t in range(NT):
                        root(24 + 16 * gr + 8 * i + 4 * t, HEADS, HD)
                    for t in range(NT):
                        drained(pool, kind, gr, t)
                        rotate(z, t)

            def level(l):
                for half in range(2):
                    s = slice(half * W, (half + 1) * W)
                    if l == 0:
                        drained(pool, "lab", half)
                    else:
                        filled(pool, "iT" if l > 1 else "iZ", l - 1, half)
                        if l == 1:
                            pool.wait_ge(S("xt_ready"), half + 1)
                    mask = cc("level")[:, l * CH:(l + 1) * CH]
                    g.tensor_tensor(mm64(Lm[:, s]), mm64(LabT[:, s]), rep(mask, 8), ALU.mult).then_inc(S("level_ready"), 1)

            def inv(l):
                if l == 0:
                    level(0)
                if l + 1 < LEVELS:
                    level(l + 1)
                else:
                    pool.wait_ge(S("iT_filled"), ledger[("iT", (l, 1))][1])
                    g.memset(stS[0], 0.0).then_inc(S("state_zero"), 1)

            stages = {"normx": normx, "angle": angle, "ck": ck, "cq": cq, "kk": kkn, "tilde": tilde, "az": az, "inv": inv}
            for st, arg in ORDER:
                if st in stages:
                    stages[st](arg)
            root(4, NT, D)
            pool.wait_ge(S("yb_ready"), 1)
            g.memset(EA[:, 2, 256:512], -UNSEL)
            g.memset(zer, 0.0).then_inc(S("zero_ready"), 1)
            pool.wait_ge(S("rmax_ready"), 1)
            g.partition_all_reduce(flag[:, 0:1], flag[:, 3:4], P, bass.bass_isa.ReduceOp.max).then_inc(S("allmax_ready"), 1)

        @block.sync
        def _(sp):
            sp.dma_start(x[:, :, :], A["x"].rearrange("o (t p) n -> p (o t) n", p=P)).then_inc(S("x_landed"), 16)
            for name in list(ROWS)[1::2]:
                sp.dma_start(row_tile(name), row_source(name)).then_inc(S("rows_landed"), 16)
            w_in, w_b, w_o, w_kv = A["w_in"][0], A["w_branch"][0], A["w_out"][0], A["w_mem_kv"][0]

            def source(kind, i):
                cols = {"r": OFF_R + W * i, "cq": OFF_CQ, "aq": W * i, "ak": A_COLS + W * i, "av": 2 * A_COLS + W * i,
                        "g0": OFF_GATE + D * i, "g1": OFF_GATE + D * i + W}
                if kind in cols:
                    c = cols[kind]
                    return w_in[:, c:c + (256 if (kind, i) == ("r", 3) else W)]
                if kind == "wb":
                    return w_b[i]
                if kind == "wo":
                    return w_o[:, W * i:W * (i + 1)]
                return w_kv[:, 0:W] if kind == "mk" else w_kv[:, W:2 * W]

            last_use = last_filled
            for n, (kind, i) in enumerate(loads):
                if n >= RING:
                    k2, idx = last_use(loads[n - RING])
                    filled(sp, k2, *idx)
                if n == 2:
                    sp.dma_start(memx, A["mem"].rearrange("o (t p) n -> p (o t) n", p=P)).then_inc(S("mem_landed"), 16)
                src = source(kind, i)
                rows_, cols_ = src.shape
                dst = ring[:, n % RING, 0:rows_ // P * cols_].rearrange("p (k n) -> p k n", n=cols_)
                sp.dma_start(dst, src.rearrange("(k p) n -> p k n", p=P)).then_inc(S(f"slot_landed{n % RING}"), 16)
            sp.wait_ge(S("yb_ready"), 1)
            sp.dma_start(b2s, A["exp_b2"][0]).then_inc(S("late_landed"), 16)
            sp.dma_start(b1raw.rearrange("p (q f) -> p q f", f=P),
                         A["exp_b1"][0].rearrange("e (c f) -> (e c) f", f=P).rearrange("(q p) f -> p q f", p=P)).then_inc(S("late_landed"), 16)
            sp.dma_start(rw, A["router_w"][0].rearrange("(k p) e -> p k e", p=P)).then_inc(S("late_landed"), 16)
            sp.dma_start(rbias, A["router_b"].to_broadcast([P, E])).then_inc(S("late_landed"), 16)

            def expert(e, k, first=False):
                w1 = A["exp_w1"][0, bass.ds(e, 1), :, :].rearrange("o (k p) n -> p (o k) n", p=P)
                w2 = A["exp_w2"][0, bass.ds(e, 1), :, :].rearrange("o (k p) n -> p (o k) n", p=P)
                for s in range(SLOTS):
                    if first and s < RING:
                        k2, idx = last_use(loads[[i for i in range(len(loads)) if i % RING == s][-1]])
                        filled(sp, k2, *idx)
                    elif not first:
                        sp.wait_ge(S(f"slot_used{s}"), k)
                    if s < 4:
                        src = w1[:, :, s * W:(s + 1) * W]
                        dst = ring[:, s, :].rearrange("p (k n) -> p k n", n=W)
                    else:
                        src = w2[:, 4 * (s - 4):4 * (s - 3), :]
                        dst = ring[:, s, :].rearrange("p (k n) -> p k n", n=D)
                    sp.dma_start(dst, src).then_inc(S(f"slot_landed{s}"), 16)

            expert(0, 0, first=True)
            with sp.Fori(1, E) as e:
                expert(e, e)
            sp.wait_ge(S("flag_ready"), 1)
            more = sp.value_load(flagi[0:1, 0:1], min_val=0, max_val=1)
            with sp.If(more > 0):
                with sp.Fori(1, T // CAP) as r:
                    with sp.Fori(0, E) as e:
                        expert(e, r * E + e)
            sp.wait_ge(S("all_added"), 1)
            sp.dma_start(out.rearrange("o (t p) n -> p (o t) n", p=P), x[:, :, :]).then_inc(S("out_written"), 16)
            sp.wait_ge(S("out_written"), 16)


ORDER_ATTN = [a for s, a in ORDER if s == "attn_s"]
ORDER_GATES = [a for s, a in ORDER if s == "gates"]


def last_filled(load):
    kind, i = load
    if kind == "r":
        return "rz", ((3, 7, 11, 13)[i],)
    if kind in ("mk", "mv", "cq"):
        return {"mk": "ck", "mv": "cv", "cq": "cq"}[kind], (NT - 1,)
    if kind in ("aq", "ak", "av"):
        return kind, (i, NT - 1)
    if kind == "wo":
        return "wo", (NT - 1, i)
    if kind == "wb":
        return "pj", (i, KC - 1)
    return "gz", (i, 3 if kind == "g0" else 7)


def shape_constants():
    p = np.arange(P)[:, None]
    c = np.zeros((P, NCONST), np.float32)

    def put(name, val):
        a, n = CONST[name]
        c[:, a:a + n] = val

    j = np.arange(P)[None, :]
    put("ident", p == j)
    put("jblk", p // RD == j // RD)
    am = []
    for window, dil in GROUPS:
        same = (p - j) % dil == 0
        span = window // dil
        am.append(np.where(same & ((P + p - j) <= span * dil), 0, NEG))
        am.append(np.where(same & (j <= p) & ((p - j) <= span * dil), 0, NEG))
    put("amask", np.concatenate(am, 1))
    s, t = np.arange(P)[:, None] % CH, np.arange(CH)[None, :]
    put("strict", t > s)
    put("incl", t >= s)
    put("level", np.concatenate([(s >> (i + 1) == t >> (i + 1)) & ((t >> i) & 1 == 1) & ((s >> i) & 1 == 0)
                                 for i in range(LEVELS)], 1))
    put("eye", s == t)
    put("reset", (np.arange(T) % CH != 0)[None, :])
    put("earlier", p < j)
    put("ones", 1.0)
    put("iota", np.arange(CAP)[None, :])
    put("invf", np.float32(THETA) ** (-np.arange(HALF, dtype=np.float32) / np.float32(HALF)))
    return c


NAMES = ["x", "mem", "positions", "norm_mix", "w_in", "b_gate", "a_q_gain", "a_k_gain", "r_mu", "r_w0", "r_w2", "r_a0",
         "r_a2", "r_g2", "r_k_k", "r_k_a", "r_r_k", "r_ln_w", "r_ln_b", "mem_norm", "w_mem_kv", "c_q_gain", "c_k_gain",
         "w_branch", "w_out", "norm_ffn", "router_w", "router_b", "exp_w1", "exp_b1", "exp_w2", "exp_b2"]


def kernel(**inputs):
    import concourse.bacc as bacc
    from concourse.bass_utils import run_bass_kernel_spmd

    nc = bacc.Bacc("TRN2", target_bir_lowering=False, num_devices=1)
    arrays = {f"in_{n}": np.ascontiguousarray(inputs[n]) for n in NAMES}
    arrays["in_consts"] = shape_constants()
    aps = {n[3:]: nc.dram_tensor(n, a.shape, mybir.dt.from_np(a.dtype), kind="ExternalInput").ap()
           for n, a in arrays.items()}
    out = nc.dram_tensor("out", (1, T, D), F32, kind="ExternalOutput").ap()
    build(nc, aps, out)
    r = run_bass_kernel_spmd(nc, [arrays], core_ids=[0])
    return r.results[0]["out"]
```

```python
import math
from contextlib import ExitStack

import concourse.bass as bass
from concourse import mybir
from concourse.alu_op_type import AluOpType as ALU
import numpy as np

F32 = mybir.dt.float32
I32 = mybir.dt.int32
ACT = mybir.ActivationFunctionType
AX = mybir.AxisListType.X

P = 128
D = 1024
T = 256
NT = T // P
KC = D // P
W = 512
HEADS, HD = 4, 128
GROUPS = ((128, 1), (512, 4), (2048, 16))
NG = len(GROUPS)
MEM = 256
RH, RD = 8, 64
PAIRS = RH // 2
CH = 64
NCH = T // CH
LEVELS = 6
NM = PAIRS * NCH
E, TOPK, DFF = 32, 4, 1024
CAP = 64
ROT = HD // 4
HALF = ROT // 2
THETA = 500000.0
EPS = 1e-6
GN_EPS = 64e-5
ALPHA, LIMIT = 1.702, 7.0
SCALE = HD ** -0.5
NEG = -1e30
LOGC = -math.exp(-0.5)
UNSEL = 1000.0

A_COLS = NG * HEADS * HD
OFF_R = 3 * A_COLS
R_COLS = 3 * RH * RD + 2 * 64 + 128
OFF_CQ = OFF_R + R_COLS
OFF_GATE = OFF_CQ + W

ROWS = {}
for _n, _c in (("norm_mix", 8), ("b_gate", 24), ("r_mu", 14), ("r_w0", 4), ("r_a0", 4), ("r_k_k", 4), ("r_k_a", 4),
               ("r_r_k", 4), ("r_ln_w", 4), ("r_ln_b", 4), ("mem_norm", 8), ("norm_ffn", 8)):
    ROWS[_n] = (sum(c for _, c in ROWS.values()), _c)
NROWS = sum(c for _, c in ROWS.values())

CONST = {}
for _n, _c in (("ident", 128), ("jblk", 128), ("amask", NG * 256), ("strict", CH), ("incl", CH), ("level", LEVELS * CH),
               ("eye", CH), ("reset", T), ("earlier", 128), ("ones", 128), ("iota", CAP), ("invf", HALF)):
    CONST[_n] = (sum(c for _, c in CONST.values()), _c)
NCONST = sum(c for _, c in CONST.values())

ORDER = [("vec", 0), ("normx", 0), ("rz", 0), ("angle", 0), ("rz", 1), ("rz", 2), ("rz", 3), ("normm", 0), ("kk_raw", 0), ("lora", 0),
         ("kk", 0), ("ck", 0), ("cv", 0), ("bonus", 0), ("tilde", 0), ("cq", 0), ("tok", 0), ("ckq_T", 0), ("attn_s", 3),
         ("L", 0), ("attn_t", 3), ("gates", (2, 0)), ("inv_a", 0), ("gates", (2, 1)), ("inv_a", 1), ("gates", (2, 2)), ("inv_b", 1),
         ("gates", (2, 3)), ("inv_a", 2), ("aq", 0), ("inv_b", 2), ("ak", 0), ("inv_a", 3), ("av", 0), ("inv_b", 3),
         ("attn_s", 0), ("inv_a", 4), ("attn_t", 0), ("inv_b", 4), ("aq", 1), ("inv_a", 5), ("ak", 1), ("inv_b", 5),
         ("av", 1), ("seq", 0), ("attn_s", 1), ("seq", 1), ("attn_t", 1), ("seq", 2), ("aq", 2), ("seq", 3), ("ak", 2),
         ("gn", 0), ("av", 2), ("gn2", 0), ("attn_s", 2), ("gates", (1, 0)), ("gates", (1, 1)), ("attn_t", 2),
         ("gates", (1, 2)), ("gates", (1, 3)), ("outA", 0), ("gates", (0, 0)), ("gates", (0, 1)), ("gates", (0, 2)),
         ("gates", (0, 3)), ("wo", 0)]
NORMS = ["x", "mem"] + [("ck", t) for t in range(NT)] + [("cq", t) for t in range(NT)] + \
    [(k, g, t) for g in range(NG) for k in "qk" for t in range(NT)] + [("ffn", t) for t in range(NT)]


def weight_loads():
    out = [("r", i) for i in range(4)] + [("mk", 0), ("mv", 0), ("cq", 0)]
    for st, a in ORDER:
        if st in ("aq", "ak", "av"):
            out += [(st, a)]
        if st == "gates":
            b, part = a
            out += {0: [("g0", b), ("wb", b)], 2: [("g1", b)]}.get(part, [])
    return out + [("wo", 0), ("wo", 1)]


RING = 4
PIECES = 6
SLOTS = 8
GROUP = 4
TURNS = GROUP * PIECES // SLOTS
QUADS = E // GROUP


def build(nc, A, out):
    ctx = ExitStack()
    with ctx:
        def sb(name, shape, dt=F32):
            return ctx.enter_context(nc.sbuf_tensor(name, shape, dt))

        sems = {}

        def S(name):
            if name not in sems:
                sems[name] = ctx.enter_context(nc.semaphore(name))
            return sems[name]

        ring = sb("ring", [P, PIECES, 4096])
        const = sb("const", [P, NCONST])
        gains = sb("gains", [P, 4, HD])
        x = sb("x", [P, NT, D])
        hT = sb("hT", [P, KC, T])
        A1 = sb("A1", [P, 6, 1024])
        PY = sb("PY", [P, 4096])
        PP, yT = PY[:, 0:3072], PY[:, 3072:4096].rearrange("p (h t) -> p h t", t=T)
        merged = sb("merged", [P, KC, T])
        EA = sb("EA", [P, 8, 1024])
        vecT = sb("vecT", [P, NROWS])
        ajunk = sb("ajunk", [P, W])
        omm = sb("omm", [P, 14])
        omka = sb("omka", [P, 4])
        ssq = sb("ssq", [P, 80])
        rst = sb("rst", [P, 80])
        negh = sb("negh", [P, 16])
        trig = sb("trig", [P, NT, 2 * ROT])
        rotb = sb("rotb", [P, 2, HEADS, ROT])
        posi = sb("posi", [P, NT], I32)
        posf = sb("posf", [P, NT])
        ePT = sb("ePT", [P, PAIRS, NCH])
        mx = sb("mx", [P, 6, NT, HEADS])
        lsum = sb("lsum", [P, 2, NT, HEADS])
        flag = sb("flag", [P, 4])
        flagi = sb("flagi", [P, 1], I32)
        small = sb("small", [P, NT, 8])
        banks = [ctx.enter_context(nc.psum_tensor(f"bank{i}", [P, W], F32)) for i in range(8)]

        def cc(name, *shape):
            a, n = CONST[name]
            return const[:, a:a + n]

        ident = cc("ident")

        def vcol(name, i=0, n=1):
            a = ROWS[name][0]
            return vecT[:, a + i:a + i + n]

        def rep(ap, n):
            return ap.unsqueeze(1).to_broadcast([ap.shape[0], n, ap.shape[1]])

        def each(ap, n):
            return ap.unsqueeze(2).to_broadcast([ap.shape[0], ap.shape[1], n])

        def row_tile(name):
            r0, n = ROWS[name]
            return rows[r0:r0 + n, :]

        def row_source(name):
            if name == "r_r_k":
                return A[name].rearrange("o (a c) b -> (o a) (c b)", c=2)
            return A[name].rearrange("o (a b) -> (o a) b", b=P)

        FA = ring[:, RING:PIECES, :].rearrange("p a (b c) -> p (a b) c", c=1024)

        def ch(ap):
            return ap.rearrange("p (a t) -> p a t", t=T)

        def mm64(ap):
            return ap.rearrange("p (m t) -> p m t", t=CH)

        r_, k_, v_, bv = FA[:, 0, :], FA[:, 1, :], FA[:, 2, :], FA[:, 4, :]
        wag = FA[:, 3, 0:2 * T].rearrange("p (a t) -> p a t", t=T)
        w2a, g2w = EA[:, 0, 0:W], EA[:, 0, W:2 * W]
        sgw, cum, a_, g_, kk, tmp6, tmp7 = (EA[:, i, :] for i in range(1, 8))
        at_, bt_, eN = FA[:, 5, :], EA[:, 7, :], FA[:, 6, :]
        Vt, Kt, Bt = EA[:, 1, :], EA[:, 2, :], EA[:, 3, :]
        LabT, LakT, LrbT, LrkT = EA[:, 5, :], EA[:, 6, :], EA[:, 0, :], FA[:, 6, :]
        XT, X, Tm, Lm = EA[:, 7, :], FA[:, 1, :], FA[:, 2, :], FA[:, 7, :]
        stS = [FA[:, 7, 0:256], FA[:, 7, 768:1024]]
        Rb, Ub = FA[:, 7, 256:512], FA[:, 7, 512:768]
        yB = FA[:, 3, :]
        gnd, gnq, gnr = FA[:, 1, :], FA[:, 2, :], EA[:, 5, :]
        zq, zk = A1[:, 0, :].rearrange("p (t n) -> p t n", t=NT), A1[:, 1, :].rearrange("p (t n) -> p t n", t=NT)
        qT, kT = ch(A1[:, 2, :]), ch(A1[:, 3, :])
        vv, O = A1[:, 4, :].rearrange("p (t n) -> p t n", t=NT), A1[:, 5, :].rearrange("p (t n) -> p t n", t=NT)
        hx = PP[:, 0:2048].rearrange("p (t n) -> p t n", t=NT)
        memx = A1[:, 0:2, :]
        rows = A1[:, 2, 0:P]
        memT = merged
        sg = [A1[:, 0, 0:T], A1[:, 0, T:2 * T]]
        gp = [A1[:, 1, 0:T], A1[:, 1, T:2 * T]]

        loads = weight_loads()
        load_no = {n: i for i, n in enumerate(loads)}
        base = [sum(1 for i in range(len(loads)) if i % RING == s) if s < RING else 0 for s in range(SLOTS)]

        def weights(eng, name):
            i = load_no[name]
            eng.wait_ge(S(f"slot_landed{i % RING}"), 16 * (i // RING + 1))
            return ring[:, i % RING, :]

        slots = [ring[:, s, :] for s in range(PIECES)] + [A1[:, 2:6, :].rearrange("p a b -> p (a b)"), PY[:, :]]

        def piece_slot(j, s):
            return (PIECES * j + s) % SLOTS

        def piece_no(g, j, s):
            return TURNS * g + (PIECES * j + s) // SLOTS

        def piece(eng, g, j, s):
            i = piece_slot(j, s)
            eng.wait_ge(S(f"slot_landed{i}"), 16 * base[i] + 16 * piece_no(g, j, s) + 16)
            return slots[i]

        def piece_used(ins, j, s):
            ins.then_inc(S(f"slot_used{piece_slot(j, s)}"), 1)

        def products(eng, g, j, s):
            reached(eng, f"slot_used{piece_slot(j, s)}", piece_no(g, j, s) + 1)

        family = {"mT": "hT", "nT": "hT", "kt": "vt", "bt": "vt", "lak": "lab", "lrb": "lab", "lrk": "lab", "lw": "lora",
                  "la": "lora", "lg": "lora", "ck": "qk", "cq": "qk", "aq": "qk", "ak": "qk", "av": "cv", "ckT": "qkT",
                  "cqT": "qkT", "aqT": "qkT", "akT": "qkT", "bn": "gn", "gm": "gn", "gv": "gn"}
        ledger, by_kind, in_bank = {}, {}, []

        def Filled(kind):
            return S(f"{family.get(kind, kind)}_filled")

        def Drained(kind):
            return S(f"{family.get(kind, kind)}_drained")

        def filled(eng, kind, *idx):
            b, n = ledger[(kind, idx)]
            eng.wait_ge(Filled(kind), n)
            return banks[b]

        def drained(eng, kind, *idx):
            eng.wait_ge(Drained(kind), ledger[(kind, idx)][1])

        def tile_parts(g):
            full = [(t, p, 2 * p, 2, 256, 0) for t in range(NT) for p in range(2)]
            return full if g == NG else [(0, 0, 0, 4, 128, 0)] + full[2:]

        def prob(g, t):
            if g < NG:
                nk = 128 * (t + 1)
                pr = PP[:, 512 * t:512 * t + 4 * nk].rearrange("p (h k) -> p h k", h=HEADS)
                pt = PP[:, 1536 + 512 * t:1536 + 512 * t + 4 * nk].rearrange("p (h b k) -> p h b k", h=HEADS, k=P)
            else:
                pr = (PP[:, 0:1024] if t == 0 else A1[:, 0, :]).rearrange("p (h k) -> p h k", h=HEADS)
                pt = (PP[:, 1024:2048] if t == 0 else A1[:, 1, :]).rearrange("p (h b k) -> p h b k", h=HEADS, k=P)
            return pr, pt

        def reached(eng, name, value):
            if not isinstance(value, int) or value > 0:
                eng.wait_ge(S(name), value)

        b1T, b1raw = EA[:, 1, 0:W], EA[:, 1, W:2 * W]
        rw = EA[:, 2, 0:KC * E].rearrange("p (k e) -> p k e", e=E)
        rank = EA[:, 2, 256:256 + 2 * (E + 1)].rearrange("p (t e) -> p t e", t=NT)
        gate = EA[:, 2, 384:384 + 2 * (E + 1)].rearrange("p (t e) -> p t e", t=NT)
        rbias = EA[:, 2, 512:512 + E]
        lgt = EA[:, 2, 576:576 + 2 * E].rearrange("p (t e) -> p t e", t=NT)
        sel = EA[:, 2, 640:640 + 2 * E].rearrange("p (t e) -> p t e", t=NT)
        eqs = EA[:, 2, 704:704 + 2 * E].rearrange("p (t e) -> p t e", t=NT)
        cnt = EA[:, 2, 768:768 + 2 * E].rearrange("p (t e) -> p t e", t=NT)
        tie = EA[:, 2, 832:832 + 2 * E].rearrange("p (t e) -> p t e", t=NT)
        zer = EA[:, 2, 896:896 + E]
        G = EA[:, 3, 0:2 * CAP].rearrange("p (t c) -> p t c", t=NT)
        Gw = EA[:, 0, 0:4 * CAP].rearrange("p (t c) -> p t c", t=NT)
        GTw = EA[:, 3, 256:512]
        xgT = EA[:, 3, 512:1024].rearrange("p (k c) -> p k c", c=CAP)
        glu, sig = EA[:, 4, 0:W], EA[:, 4, W:2 * W]
        lin, actT = EA[:, 5, 0:W], EA[:, 5, W:2 * W]
        ysb = EA[:, 6, 0:W]
        usb = A1[:, 0, :]
        xn = hT[:, :, :].rearrange("p a b -> p (a b)").rearrange("p (t n) -> p t n", t=NT)
        hnT = A1[:, 0:2, :].rearrange("p a (b t) -> p (a b) t", t=T)
        XG, U0, U1, TU, YB, C0, C1, GB = banks
        LO, HI = slice(0, CAP), slice(CAP, 2 * CAP)

        block = ctx.enter_context(nc.Block())

        @block.tensor
        def _(pe):
            mm = nc.tensor.matmul

            def claim(kind, *idx):
                b = len(in_bank) % 8
                if len(in_bank) >= 8:
                    drained(pe, in_bank[-8][0], *in_bank[-8][1])
                f = family.get(kind, kind)
                by_kind[f] = by_kind.get(f, 0) + 1
                ledger[(kind, idx)] = (b, by_kind[f])
                in_bank.append((kind, idx))
                return banks[b]

            def done(ins, kind):
                ins.then_inc(Filled(kind), 1)

            def vec(_):
                pe.wait_ge(S("ident_landed"), 16)
                pe.wait_ge(S("rows_landed"), 16 * len(ROWS))
                done(nc.tensor.transpose(claim("vec")[:, 0:NROWS], rows[0:NROWS, :], ident[0:NROWS, 0:NROWS]), "vec")

            def turn(kind, src, sem):
                for t in range(NT):
                    pe.wait_ge(S(sem), t + 1)
                    turn_tile(kind, src, t)

            def turn_tile(kind, src, t):
                for half in range(2):
                    bank = claim(kind, t, half)
                    for j in range(4):
                        c = 4 * half + j
                        ins = nc.tensor.transpose(bank[:, j * P:(j + 1) * P], src[:, t, c * P:(c + 1) * P], ident)
                    done(ins, kind)

            def channel_chunk(bank, w, c, rhs, nk=KC, width=W):
                for kc in range(nk):
                    ins = mm(bank[:, 0:T], w[:, kc * width + c * P:kc * width + (c + 1) * P], rhs[:, kc, :],
                             start=(kc == 0), stop=(kc == nk - 1))
                return ins

            def rz(i):
                if i == 0:
                    for t in range(NT):
                        for half in range(2):
                            drained(pe, "hT", t, half)
                w = weights(pe, ("r", i))
                width = W if i < 3 else 256
                for c in range(width // P):
                    bank = claim("rz", 4 * i + c)
                    ins = channel_chunk(bank, w, c, hT, width=width)
                    done(ins, "rz")

            def lora(_):
                pe.wait_ge(S("lora_landed"), 48)
                pe.wait_ge(S("wlo_ready"), 2)
                drained(pe, "rz", 13)
                for p in range(PAIRS):
                    for kind, lhs, rhs in (("lw", w2a[0:64, p * P:(p + 1) * P], wag[0:64, 0, :]),
                                           ("la", w2a[64:128, p * P:(p + 1) * P], wag[64:128, 0, :]),
                                           ("lg", g2w[:, p * P:(p + 1) * P], wag[:, 1, :])):
                        done(mm(claim(kind, p)[:, 0:T], lhs, rhs, start=True, stop=True), kind)

            def token_tile(kind, t, src, w):
                bank = claim(kind, t)
                for kc in range(KC):
                    ins = mm(bank[:, :], src[:, kc, t * P:(t + 1) * P], w[:, kc * W:(kc + 1) * W],
                             start=(kc == 0), stop=(kc == KC - 1))
                done(ins, kind)

            def heads_turn(kind, srckind, src):
                for t in range(NT):
                    if srckind[0] == "A":
                        pe.wait_ge(S("rot_done"), srckind[1] * NT + t + 1)
                    else:
                        drained(pe, srckind[1], t)
                    bank = claim(kind, t)
                    for h in range(HEADS):
                        ins = nc.tensor.transpose(bank[:, h * P:(h + 1) * P], src[:, t, h * P:(h + 1) * P], ident)
                    done(ins, kind)

            def ck(_):
                for t in range(NT):
                    for half in range(2):
                        drained(pe, "mT", t, half)
                w = weights(pe, ("mk", 0))
                for t in range(NT):
                    token_tile("ck", t, memT, w)

            def cv(_):
                w = weights(pe, ("mv", 0))
                for t in range(NT):
                    token_tile("cv", t, memT, w)

            def cq(_):
                w = weights(pe, ("cq", 0))
                for t in range(NT):
                    token_tile("cq", t, hT, w)

            def ckq_T(_):
                heads_turn("ckT", ("C", "ck"), zk)
                heads_turn("cqT", ("C", "cq"), zq)

            def kkn(_):
                pe.wait_ge(S("const_landed"), 16)
                for half in range(2):
                    pe.wait_ge(S("kksq_ready"), half + 1)
                    done(mm(claim("kn", half)[:, :], cc("jblk"), tmp6[:, half * W:(half + 1) * W], start=True, stop=True), "kn")

            def bonus(_):
                pe.wait_ge(S("rkk_ready"), 1)
                for half in range(2):
                    done(mm(claim("bn", half)[:, :], cc("jblk"), tmp6[:, half * W:(half + 1) * W], start=True, stop=True), "bn")

            def head64(bank, col, pairs_of):
                for j, (lhs, rhs, n, first, last) in enumerate(pairs_of):
                    for h in range(2):
                        s = slice(64 * h, 64 * h + 64)
                        ins = mm(bank[s, col:col + n], lhs[s, :], rhs[s, :], start=first, stop=last,
                                 skip_group_check=True)
                return ins

            def tok(_):
                pe.wait_ge(S("tilde_ready"), 1)
                for kind, src in (("vt", v_), ("kt", k_), ("bt", bt_)):
                    for half in range(2):
                        bank = claim(kind, half)
                        for m in range(8):
                            c = half * W + m * CH
                            ins = head64(bank, m * CH, [(src[:, c:c + CH], cc("eye"), CH, m == 0, m == 7)])
                        done(ins, kind)

            def L(_):
                for kind, lhs, rhs in (("lab", bt_, at_), ("lak", k_, at_), ("lrb", bt_, r_), ("lrk", k_, r_)):
                    for half in range(2):
                        bank = claim(kind, half)
                        for m in range(8):
                            c = half * W + m * CH
                            ins = head64(bank, m * CH, [(lhs[:, c:c + CH], rhs[:, c:c + CH], CH, m == 0, m == 7)])
                        done(ins, kind)

            def batch(kind, l, half, lhs, rhs):
                bank = claim(kind, l, half)
                for m in range(8):
                    c = half * W + m * CH
                    rr = cc("eye") if rhs is None else rhs[:, c:c + CH]
                    ins = head64(bank, m * CH, [(lhs[:, c:c + CH], rr, CH, m == 0, m == 7)])
                done(ins, kind)

            def inv(l):
                for half in range(2):
                    pe.wait_ge(S("level_ready"), 2 * l + half + 1)
                    if l > 0:
                        drained(pe, "iZ" if l == 1 else "iX", l - 1, half)
                    batch("iT" if l else "iZ", l, half, Lm, X if l else None)

            def inv_b(l):
                for half in range(2):
                    drained(pe, "iT", l, half)
                    if l == 1:
                        pe.wait_ge(S("xt_ready"), 2)
                    else:
                        drained(pe, "iXT", l - 1, half)
                    if l < LEVELS - 1:
                        batch("iX", l, half, XT, Tm)
                    batch("iXT", l, half, Tm, XT)

            def pr(ap, p, n=CH):
                return ap[:, p * n:(p + 1) * n]

            def seq(c):
                bank = claim("sR", c)
                for k in ("lab", "lak", "lrb", "lrk"):
                    drained(pe, k, 1)
                for k in ("vt", "kt", "bt"):
                    drained(pe, k, 1)
                for p in range(PAIRS):
                    m = p * NCH + c
                    ins = head64(bank, p * CH, [(pr(LakT, m), pr(Vt, m), CH, p == 0, False)])
                if c == 0:
                    pe.wait_ge(S("state_zero"), 1)
                else:
                    drained(pe, "sS", c - 1)
                for p in range(PAIRS):
                    m = p * NCH + c
                    ins = head64(bank, p * CH, [(pr(at_, m), pr(stS[c % 2], p), CH, False, p == PAIRS - 1)])
                done(ins, "sR")
                bank = claim("sS", c)
                for p in range(PAIRS):
                    m = p * NCH + c
                    head64(bank, p * CH, [(pr(Kt, m), pr(Vt, m), CH, p == 0, False)])
                ubank = claim("sU", c)
                drained(pe, "iXT", LEVELS - 1, 0)
                drained(pe, "iXT", LEVELS - 1, 1)
                drained(pe, "sR", c)
                for p in range(PAIRS):
                    m = p * NCH + c
                    ins = head64(ubank, p * CH, [(pr(XT, m), pr(Rb, p), CH, p == 0, p == PAIRS - 1)])
                done(ins, "sU")
                ybank = claim("sY", c)
                for p in range(PAIRS):
                    m = p * NCH + c
                    head64(ybank, p * CH, [(pr(Vt, m), pr(LrkT, m), CH, p == 0, False),
                                           (pr(stS[c % 2], p), pr(r_, m), CH, False, False)])
                drained(pe, "sU", c)
                for p in range(PAIRS):
                    m = p * NCH + c
                    ins = head64(bank, p * CH, [(pr(Bt, m), pr(Ub, p), CH, False, p == PAIRS - 1)])
                done(ins, "sS")
                for p in range(PAIRS):
                    m = p * NCH + c
                    ins = head64(ybank, p * CH, [(pr(Ub, p), pr(LrbT, m), CH, False, p == PAIRS - 1)])
                done(ins, "sY")

            def gn(_):
                for c in range(NCH):
                    drained(pe, "sY", c)
                for half in range(2):
                    done(mm(claim("gm", half)[:, :], cc("jblk"), yB[:, half * W:(half + 1) * W], start=True, stop=True), "gm")

            def gn2(_):
                pe.wait_ge(S("gnsq_ready"), 1)
                for half in range(2):
                    done(mm(claim("gv", half)[:, :], cc("jblk"), gnq[:, half * W:(half + 1) * W], start=True, stop=True), "gv")

            def az(kind, g):
                w = weights(pe, (kind, g))
                for t in range(NT):
                    bank = claim(kind, g, t)
                    for kc in range(KC):
                        ins = mm(bank[:, :], hT[:, kc, t * P:(t + 1) * P], w[:, kc * W:(kc + 1) * W],
                                 start=(kc == 0), stop=(kc == KC - 1))
                    done(ins, kind)

            def attn_s(g):
                if g < NG:
                    for i, (kind, src) in enumerate((("aqT", zq), ("akT", zk))):
                        for t in range(NT):
                            pe.wait_ge(S("rot_done"), (g * 2 + i) * NT + t + 1)
                            bank = claim(kind, g, t)
                            for h in range(HEADS):
                                ins = nc.tensor.transpose(bank[:, h * P:(h + 1) * P], src[:, t, h * P:(h + 1) * P], ident)
                            done(ins, kind)
                for t in range(NT):
                    if g < NG:
                        drained(pe, "aqT", g, t)
                        drained(pe, "akT", g, t)
                    else:
                        drained(pe, "cqT", t)
                        drained(pe, "ckT", t)
                for t, part, h0, nh, nk, k0 in tile_parts(g):
                    bank = claim("sc", g, t, part)
                    for h in range(h0, h0 + nh):
                        ins = mm(bank[:, (h - h0) * nk:(h - h0 + 1) * nk], qT[:, h, t * P:(t + 1) * P], kT[:, h, k0:k0 + nk],
                                 start=True, stop=True)
                    done(ins, "sc")

            def attn_t(g):
                for t, part, h0, nh, nk, k0 in tile_parts(g):
                    pr_, _ = prob(g, t)
                    pe.wait_ge(S("probs_ready"), NT * ORDER_ATTN.index(g) + t + 1)
                    bank = claim("pT", g, t, part)
                    i = 0
                    for h in range(h0, h0 + nh):
                        for b in range(nk // P):
                            ins = nc.tensor.transpose(bank[:, i * P:(i + 1) * P], pr_[:, h, b * P:(b + 1) * P], ident)
                            i += 1
                    done(ins, "pT")
                for t in range(NT):
                    _, pt = prob(g, t)
                    parts = [p for p in tile_parts(g) if p[0] == t]
                    for p in parts:
                        drained(pe, "pT", g, t, p[1])
                    if g < NG:
                        for tt in range(NT):
                            drained(pe, "av", g, tt)
                    else:
                        for tt in range(NT):
                            drained(pe, "cv", tt)
                    nb = parts[0][4] // P
                    bank = claim("pv", g, t)
                    for h in range(HEADS):
                        for b in range(nb):
                            ins = mm(bank[:, h * P:(h + 1) * P], pt[:, h, b, :], vv[:, b, h * P:(h + 1) * P],
                                     start=(b == 0), stop=(b == nb - 1))
                    done(ins, "pv")
                if g == NG:
                    out_heads(1)

            def out_heads(n):
                for t in range(NT):
                    pe.wait_ge(S("o_ready"), NT * (n - 1) + t + 1)
                    bank = claim("oT", n, t)
                    for h in range(HEADS):
                        ins = nc.tensor.transpose(bank[:, h * P:(h + 1) * P], O[:, t, h * P:(h + 1) * P], ident)
                    done(ins, "oT")

            def gates(part):
                b, i = part
                wb = weights(pe, ("wb", b))
                wg = weights(pe, (f"g{i // 2}", b))
                for c in (2 * i, 2 * i + 1):
                    bank = claim("gz", b, c)
                    done(channel_chunk(bank, wg, c % 4, hT), "gz")
                    if c == 0:
                        if b == 1:
                            pe.wait_ge(S("yb_ready"), 1)
                        else:
                            for t in range(NT):
                                drained(pe, "oT", 1 if b == 2 else 2, t)
                    bank = claim("pj", b, c)
                    done(channel_chunk(bank, wb, c, yT, nk=HEADS, width=D), "pj")

            def wo(_):
                pe.wait_ge(S("merged_ready"), (NG - 1) * KC)
                for t in range(NT):
                    for half in range(2):
                        w = weights(pe, ("wo", half))
                        bank = claim("wo", t, half)
                        for kc in range(KC):
                            ins = mm(bank[:, :], merged[:, kc, t * P:(t + 1) * P], w[:, kc * W:(kc + 1) * W],
                                     start=(kc == 0), stop=(kc == KC - 1))
                        done(ins, "wo")
                        if t:
                            (turn_x, logits)[half](t - 1)

            def turn_x(t):
                for half in range(2):
                    drained(pe, "wo", t, half)
                turn_tile("nT", x, t)

            def logits(t):
                for half in range(2):
                    drained(pe, "nT", t, half)
                pe.wait_ge(S("late_landed"), 16 * 5)
                bank = claim("rl", t)
                for kc in range(KC):
                    ins = mm(bank[:, 0:E], hnT[:, kc, t * P:(t + 1) * P], rw[:, kc, :], start=(kc == 0), stop=(kc == KC - 1))
                done(ins, "rl")

            stages = {"vec": vec, "normx": lambda _: turn("hT", hx, "h_ready"), "normm": lambda _: turn("mT", memx, "memn_ready"),
                      "rz": rz, "lora": lora, "ckq_T": ckq_T, "ck": ck, "cv": cv, "cq": cq, "kk": kkn, "bonus": bonus, "tok": tok, "L": L,
                      "inv_a": inv, "inv_b": inv_b, "seq": seq, "gn": gn, "gn2": gn2, "av": lambda g: az("av", g),
                      "aq": lambda g: az("aq", g), "ak": lambda g: az("ak", g), "attn_s": attn_s, "attn_t": attn_t,
                      "outA": lambda _: out_heads(2), "gates": gates, "wo": wo}
            for st, arg in ORDER:
                if st in stages:
                    stages[st](arg)

            bank = claim("b1")
            for q in range(4):
                ins = nc.tensor.transpose(bank[:, q * P:(q + 1) * P], b1raw[:, q * P:(q + 1) * P], ident)
            done(ins, "b1")
            turn_x(NT - 1)
            logits(NT - 1)
            pe.wait_ge(S("sel_ready"), NT)
            bank = claim("rk", 0)
            done(mm(bank[:, 0:E], cc("earlier"), sel[:, 0, :], start=True, stop=True), "rk")
            bank = claim("rk", 1)
            mm(bank[:, 0:E], cc("ones"), sel[:, 0, :], start=True, stop=False)
            done(mm(bank[:, 0:E], cc("earlier"), sel[:, 1, :], start=False, stop=True), "rk")
            for kind, idx in in_bank[-8:]:
                drained(pe, kind, *idx)

            def gather(n):
                pe.wait_ge(S("G_ready"), n + 1)
                for kc in range(KC):
                    for t in range(NT):
                        ins = mm(XG[:, kc * CAP:(kc + 1) * CAP], xn[:, t, kc * P:(kc + 1) * P], G[:, t, :],
                                 start=(t == 0), stop=(t == NT - 1))
                ins.then_inc(S("xg_filled"), 1)

            def scatter(q, t):
                if t == 0:
                    pe.wait_ge(S("y_evac"), q + 1)
                    pe.wait_ge(S("gt_evac"), q + 1)
                reached(pe, "c_added", 4 * q + 2 * t)
                for half, s in enumerate((LO, HI)):
                    mm((C0, C1)[half][:, :], GTw[s, t * P:(t + 1) * P], ysb[s, :],
                       start=True, stop=True).then_inc(S("c_filled"), 1)

            def turn_u(i):
                for b in range(4):
                    ins = nc.tensor.transpose((TU, U0)[i][:, b * P:(b + 1) * P], usb[:, i * W + b * P:i * W + (b + 1) * P], ident)
                ins.then_inc(S("tu_filled"), 1)

            def expert(g, j, n):
                k = GROUP * g + j
                pe.wait_ge(S("xg_evac"), n + 1)
                reached(pe, "act_ready", k)
                for i, bank in enumerate((U0, U1)):
                    w = [piece(pe, g, j, 2 * i + h) for h in range(2)]
                    for kc in range(KC):
                        for h, s in enumerate((LO, HI)):
                            ins = mm(bank[s, :], xgT[:, kc, :], w[h][:, kc * W:(kc + 1) * W],
                                     start=(kc == 0), stop=(kc == KC - 1))
                            if kc == KC - 1:
                                piece_used(ins, j, 2 * i + h)
                scatter(n, 0)
                pe.wait_ge(S("u_evac"), 2 * k + 1)
                turn_u(0)
                pe.wait_ge(S("Gw_ready"), k + 1)
                pe.wait_ge(S("gt_evac"), n + 1)
                gather(n + 1)
                for t in range(NT):
                    ins = nc.tensor.transpose(GB[:, t * P:(t + 1) * P], Gw[:, t, :], ident)
                ins.then_inc(S("gt_filled"), 1)
                pe.wait_ge(S("u_evac"), 2 * k + 2)
                turn_u(1)
                scatter(n, 1)
                pe.wait_ge(S("act_ready"), k + 1)
                for s in range(2):
                    w = piece(pe, g, j, 4 + s)
                    for c in range(4):
                        for half, hs in enumerate((LO, HI)):
                            ins = mm(YB[hs, :], actT[:, (2 * c + s) * CAP:(2 * c + s + 1) * CAP],
                                     w[:, c * D + half * W:c * D + (half + 1) * W],
                                     start=(s + c == 0), stop=(s + c == 4))
                    piece_used(ins, j, 4 + s)

            def serve(r):
                pe.wait_ge(S("xg_evac"), r * (E + 1))
                gather(r * (E + 1))
                if isinstance(r, int):
                    pe.wait_ge(S("gate_ready"), NT)
                    for t in range(NT):
                        ins = nc.tensor.transpose(GB[:, t * P:(t + 1) * P], Gw[:, t, :], ident)
                    ins.then_inc(S("gate_turned"), 1)
                for j in range(GROUP):
                    expert(r * QUADS, j, r * (E + 1) + j)
                with pe.Fori(1, QUADS) as g:
                    for j in range(GROUP):
                        expert(r * QUADS + g, j, r * (E + 1) + GROUP * g + j)
                scatter(r * (E + 1) + E, 0)
                scatter(r * (E + 1) + E, 1)

            serve(0)
            pe.wait_ge(S("flag_ready"), 1)
            more = pe.value_load(flagi[0:1, 0:1], min_val=0, max_val=1)
            with pe.If(more > 0):
                with pe.Fori(1, T // CAP) as r:
                    serve(r)

        @block.vector
        def _(dve):
            v = nc.vector
            steps = [0]

            def link(ins):
                steps[0] += 1
                ins.then_inc(S("dve_step"), 1)
                dve.wait_ge(S("dve_step"), steps[0])

            def drain(ins, kind):
                ins.then_inc(Drained(kind), 1)

            tt, ts, stt = v.tensor_tensor, v.tensor_scalar, v.scalar_tensor_tensor

            def vec(_):
                ps = filled(dve, "vec")
                drain(v.tensor_copy(vecT[:, :], ps[:, 0:NROWS]), "vec")
                drained(dve, "vec")
                link(ts(omm[:, :], vcol("r_mu", 0, 14), -1.0, 1.0, ALU.mult, ALU.add))
                ts(omka[:, :], vcol("r_k_a", 0, 4), -1.0, 1.0, ALU.mult, ALU.add).then_inc(S("omm_ready"), 1)

            def angle(_):
                dve.wait_ge(S("pos_landed"), 16)
                dve.wait_ge(S("const_landed"), 16)
                link(v.tensor_copy(posf[:, :], posi[:, :]))
                ang = A1[:, 5, 0:NT * HALF].rearrange("p (t k) -> p t k", t=NT)
                kf = A1[:, 5, 64:64 + NT * HALF].rearrange("p (t k) -> p t k", t=NT)
                rs = A1[:, 5, 128:128 + NT * HALF].rearrange("p (t k) -> p t k", t=NT)
                rc = A1[:, 5, 192:192 + NT * HALF].rearrange("p (t k) -> p t k", t=NT)
                link(tt(ang, rep(cc("invf"), NT), each(posf[:, :], HALF), ALU.mult))
                magic = 1.5 * 2.0 ** 23
                link(ts(kf, ang, 1.0 / (2 * math.pi), None, ALU.mult))
                link(ts(kf, kf, magic, None, ALU.add))
                link(ts(kf, kf, -magic, None, ALU.add))
                rest, pieces = 2 * math.pi, []
                for bits in (5, 13, 22):
                    piece = math.floor(rest * 2.0 ** bits) / 2.0 ** bits
                    pieces.append(piece)
                    rest -= piece
                pieces.append(rest)
                for i, piece in enumerate(pieces):
                    link(stt(rs, kf, -piece, ang if i == 0 else rs, ALU.mult, ALU.add))
                link(ts(rc, rs, math.pi / 2, None, ALU.add))
                link(ts(kf, rc, math.pi, -2 * math.pi, ALU.is_gt, ALU.mult))
                link(tt(rc, rc, kf, ALU.add))
                lim = 3.1415925
                ts(rs, rs, lim, -lim, ALU.min, ALU.max)
                ts(rc, rc, lim, -lim, ALU.min, ALU.max).then_inc(S("angle_ready"), 1)

            def scaled(name, src, dst, sem, i):
                dve.wait_ge(S("rstd_ready"), NORMS.index(name) + 1)
                for t in range(NT):
                    ts(dst[:, t, :], src[:, t, :], rst[:, i + t:i + t + 1], None, ALU.mult).then_inc(S(sem), 1)

            def turned(kind, gain, dst):
                for t in range(NT):
                    turned_tile(kind, gain, dst, t)

            def turned_tile(kind, gain, dst, t):
                for half in range(2):
                    ps = filled(dve, kind, t, half)
                    drain(tt(dst[:, 4 * half:4 * half + 4, t * P:(t + 1) * P],
                             ps[:, :].rearrange("p (a b) -> p a b", b=P),
                             each(vcol(gain, 4 * half, 4), P), ALU.mult), kind)

            def normx(_):
                scaled("x", x, hx, "h_ready", 0)
                turned("hT", "norm_mix", hT)

            def normm(_):
                scaled("mem", memx, memx, "memn_ready", 2)
                turned("mT", "mem_norm", memT)

            dst_rz = [ch(r_), ch(k_), ch(v_), wag]

            def rz(i):
                for c in range(4 if i < 3 else 2):
                    n = 4 * i + c
                    ps = filled(dve, "rz", n)
                    dve.wait_ge(S("rz_scaled"), n + 1)
                    d = dst_rz[i][:, c, 1:T]
                    drain(stt(d, ps[:, 0:T - 1], vcol("r_mu", n), d, ALU.mult, ALU.add), "rz")

            def kk_raw(_):
                drained(dve, "rz", 13)
                for p in range(PAIRS):
                    ins = ts(ch(kk)[:, p, :], ch(k_)[:, p, :], vcol("r_k_k", p), None, ALU.mult)
                    if p % 2:
                        ins.then_inc(S("kk_raw"), 1)

            def kkn(_):
                drained(dve, "la", PAIRS - 1)
                for p in range(PAIRS):
                    ins = v.tensor_tensor_scan(ch(cum)[:, p, :], cc("reset"), ch(sgw)[:, p, :], 0.0, ALU.mult, ALU.add)
                ins.then_inc(S("cum_ready"), 1)
                for half in range(2):
                    drained(dve, "kn", half)
                    s = slice(half * W, (half + 1) * W)
                    link(ts(tmp7[:, s], tmp7[:, s], 1e-12, None, ALU.max))
                    link(v.reciprocal(tmp7[:, s], tmp7[:, s]))
                    link(tt(kk[:, s], kk[:, s], tmp7[:, s], ALU.mult))
                for p in range(PAIRS):
                    ins = ts(ch(tmp7)[:, p, :], ch(a_)[:, p, :], vcol("r_k_a", p), omka[:, p:p + 1], ALU.mult, ALU.add)
                link(ins)
                link(tt(k_, k_, tmp7, ALU.mult))
                for p in range(PAIRS):
                    ins = stt(ch(tmp6)[:, p, :], ch(r_)[:, p, :], vcol("r_r_k", p), ch(k_)[:, p, :], ALU.mult, ALU.mult)
                ins.then_inc(S("rkk_ready"), 1)

            def bonus(_):
                for half in range(2):
                    ps = filled(dve, "bn", half)
                    s = slice(half * W, (half + 1) * W)
                    drain(tt(bv[:, s], ps[:, :], v_[:, s], ALU.mult), "bn")

            def tilde(_):
                dve.wait_ge(S("exps_ready"), 3)
                dve.wait_ge(S("ept_ready"), 1)
                stt(at_, kk, -1.0, sgw, ALU.mult, ALU.mult)
                link(tt(bt_, kk, a_, ALU.mult))
                tt(bt_, bt_, eN, ALU.mult)
                tt(k_, k_, eN, ALU.mult)
                tt(r_, r_, cum, ALU.mult).then_inc(S("tilde_ready"), 1)

            def head_norm(kind, idx, name, gain, col, dst):
                t = idx[-1]
                ps = filled(dve, kind, *idx)
                dve.wait_ge(S("rstd_ready"), NORMS.index(name) + 1)
                for h in range(HEADS):
                    ins = stt(dst[:, t, h * HD:(h + 1) * HD], ps[:, h * HD:(h + 1) * HD],
                              rst[:, col + h:col + h + 1], gains[:, gain, :], ALU.mult, ALU.mult)
                drain(ins, kind)

            def ck(_):
                dve.wait_ge(S("gains_landed"), 64)
                for t in range(NT):
                    head_norm("ck", (t,), ("ck", t), 3, 8 + 4 * t, zk)

            def cq(_):
                for t in range(NT):
                    head_norm("cq", (t,), ("cq", t), 2, 16 + 4 * t, zq)

            def az(kind, g):
                i = ("aq", "ak").index(kind)
                if g == 0:
                    drained(dve, "pj", 2, KC - 1)
                for t in range(NT):
                    head_norm(kind, (g, t), ("qk"[i:i + 1], g, t), i, 24 + 16 * g + 8 * i + 4 * t, (zq, zk)[i])

            def attn_s(g):
                m_new, m_old = mx[:, g % 2, :, :], mx[:, (g + 1) % 2, :, :]
                n_at = ORDER_ATTN.index(g)
                for t in range(NT):
                    pr_, _ = prob(g, t)
                    parts = [p for p in tile_parts(g) if p[0] == t]
                    for _t, part, h0, nh, nk, k0 in parts:
                        ps = filled(dve, "sc", g, t, part)
                        s3 = ps[:, 0:nh * nk].rearrange("p (h k) -> p h k", k=nk)
                        if g < NG:
                            a = CONST["amask"][0] + 256 * g + (128 if t == 0 else 0)
                            drain(stt(pr_[:, h0:h0 + nh, :], s3, SCALE, rep(const[:, a:a + nk], nh), ALU.mult, ALU.add), "sc")
                        else:
                            drain(ts(pr_[:, h0:h0 + nh, :], s3, SCALE, None, ALU.mult), "sc")
                        drained(dve, "sc", g, t, part)
                    if g in (0, NG):
                        link(v.tensor_reduce(m_new[:, t, :], pr_, AX, ALU.max))
                    else:
                        link(v.tensor_reduce(mx[:, 3, t, :], pr_, AX, ALU.max))
                        link(tt(m_new[:, t, :], mx[:, 3, t, :], m_old[:, t, :], ALU.max))
                        link(tt(mx[:, 4, t, :], m_old[:, t, :], m_new[:, t, :], ALU.subtract))
                    ts(mx[:, 2, t, :], m_new[:, t, :], -1.0, None, ALU.mult).then_inc(S("max_ready"), 1)

            def attn_t(g):
                n_at = ORDER_ATTN.index(g)
                for t in range(NT):
                    ps = filled(dve, "pv", g, t)
                    dve.wait_ge(S("probs_ready"), NT * n_at + t + 1)
                    if g in (0, NG):
                        if g == 0 and t == 0:
                            for tt_ in range(NT):
                                dve.wait_ge(S("oT_filled"), ledger[("oT", (1, tt_))][1])
                        drain(v.tensor_copy(O[:, t, :], ps[:, :]), "pv")
                        link(v.tensor_copy(lsum[:, 0, t, :], lsum[:, 1, t, :]))
                    else:
                        o3 = O[:, t, :].rearrange("p (h k) -> p h k", k=HD)
                        tt(lsum[:, 0, t, :], lsum[:, 0, t, :], mx[:, 5, t, :], ALU.mult)
                        link(tt(o3, o3, each(mx[:, 5, t, :], HD), ALU.mult))
                        tt(lsum[:, 0, t, :], lsum[:, 0, t, :], lsum[:, 1, t, :], ALU.add)
                        drain(tt(O[:, t, :], O[:, t, :], ps[:, :], ALU.add), "pv")
                    drained(dve, "pv", g, t)
                    if g in (NG, NG - 1):
                        link(v.reciprocal(mx[:, 3, t, :], lsum[:, 0, t, :]))
                        o3 = O[:, t, :].rearrange("p (h k) -> p h k", k=HD)
                        tt(o3, o3, each(mx[:, 3, t, :], HD), ALU.mult).then_inc(S("o_ready"), 1)

            def gates(part):
                b, i = part
                for c in (2 * i, 2 * i + 1):
                    ps = filled(dve, "pj", b, c)
                    drained(dve, "gz", b, c)
                    if ORDER_GATES.index(b) == 0:
                        tt(merged[:, c, :], ps[:, 0:T], sg[c % 2], ALU.mult).then_inc(S("pj_drained"), 1)
                    else:
                        tt(gp[c % 2], ps[:, 0:T], sg[c % 2], ALU.mult).then_inc(S("pj_drained"), 1)
                        dve.wait_ge(S("pj_drained"), ledger[("pj", (b, c))][1])
                        tt(merged[:, c, :], merged[:, c, :], gp[c % 2], ALU.add).then_inc(S("merged_ready"), 1)

            def L(_):
                for kind, dst, mask in (("lab", LabT, "strict"), ("lak", LakT, "strict"), ("lrb", LrbT, "incl"), ("lrk", LrkT, "incl")):
                    for half in range(2):
                        ps = filled(dve, kind, half)
                        s = slice(half * W, (half + 1) * W)
                        drain(tt(mm64(dst[:, s]), mm64(ps[:, :]), rep(cc(mask), 8), ALU.mult), kind)

            def inv(l):
                if l == 0:
                    for half in range(2):
                        s = slice(half * W, (half + 1) * W)
                        dve.wait_ge(S("level_ready"), half + 1)
                        filled(dve, "lrk", 1)
                        tt(mm64(XT[:, s]), mm64(Lm[:, s]), rep(cc("eye"), 8), ALU.add).then_inc(S("xt_ready"), 1)
                        ps = filled(dve, "iZ", 0, half)
                        drain(tt(mm64(X[:, s]), mm64(ps[:, :]), rep(cc("eye"), 8), ALU.add), "iZ")

            def inv_b(l):
                for half in range(2):
                    s = slice(half * W, (half + 1) * W)
                    if l < LEVELS - 1:
                        ps = filled(dve, "iX", l, half)
                        drain(tt(X[:, s], X[:, s], ps[:, :], ALU.add), "iX")
                    ps = filled(dve, "iXT", l, half)
                    drain(tt(XT[:, s], XT[:, s], ps[:, :], ALU.add), "iXT")

            def seq(c):
                ps = filled(dve, "sR", c)
                if c == 0:
                    dve.wait_ge(S("iT_filled"), ledger[("iT", (LEVELS - 1, 1))][1])
                drain(v.tensor_copy(Rb, ps[:, 0:256]), "sR")
                ps = filled(dve, "sU", c)
                drain(v.tensor_copy(Ub, ps[:, 0:256]), "sU")
                ps = filled(dve, "sS", c)
                new = stS[(c + 1) % 2]
                if c == 0:
                    dve.wait_ge(S("state_zero"), 1)
                link(tt(new, stS[c % 2], ps[:, 0:256], ALU.add))
                drain(tt(mm64(new), mm64(new), each(ePT[:, :, c], CH), ALU.mult), "sS")
                ps = filled(dve, "sY", c)
                drain(v.tensor_copy(ch(yB)[:, :, c * CH:(c + 1) * CH], mm64(ps[:, 0:256])), "sY")

            def gn(_):
                for half in range(2):
                    ps = filled(dve, "gm", half)
                    s = slice(half * W, (half + 1) * W)
                    drain(stt(gnd[:, s], ps[:, :], -1.0 / RD, yB[:, s], ALU.mult, ALU.add), "gm")
                drained(dve, "gm", 1)
                tt(gnq, gnd, gnd, ALU.mult).then_inc(S("gnsq_ready"), 1)

            def gn2(_):
                for half in range(2):
                    ps = filled(dve, "gv", half)
                    s = slice(half * W, (half + 1) * W)
                    drain(ts(gnr[:, s], ps[:, :], 1.0 / RD, GN_EPS, ALU.mult, ALU.add), "gv")
                dve.wait_ge(S("gn_root"), 1)
                link(v.reciprocal(gnr, gnr))
                link(tt(gnd, gnd, gnr, ALU.mult))
                for p in range(PAIRS):
                    ins = ts(ch(gnd)[:, p, :], ch(gnd)[:, p, :], vcol("r_ln_w", p), vcol("r_ln_b", p), ALU.mult, ALU.add)
                link(ins)
                link(tt(gnd, gnd, bv, ALU.add))
                dve.wait_ge(S("pj_filled"), ledger[("pj", (2, KC - 1))][1])
                tt(yT[:, :, :].rearrange("p a b -> p (a b)"), gnd, g_, ALU.mult).then_inc(S("yb_ready"), 1)

            def wo(_):
                for t in range(NT):
                    for half in range(2):
                        ps = filled(dve, "wo", t, half)
                        s = slice(half * W, (half + 1) * W)
                        drain(tt(x[:, t, s], x[:, t, s], ps[:, :], ALU.add), "wo")
                        if t:
                            (turned_x, choose)[half](t - 1)

            def turned_x(t):
                turned_tile("nT", "norm_ffn", hnT, t)

            def choose(t):
                dve.wait_ge(S("late_landed"), 16 * 5)
                dve.wait_ge(S("zero_ready"), 1)
                dve.wait_ge(S("rstd_ready"), NORMS.index(("ffn", t)) + 1)
                ps = filled(dve, "rl", t)
                top = small[:, t, :]
                drain(stt(lgt[:, t, :], ps[:, 0:E], rst[:, 4 + t:5 + t], rbias, ALU.mult, ALU.add), "rl")
                drained(dve, "rl", t)
                link(v.max(top, lgt[:, t, :]))
                link(ts(sel[:, t, :], lgt[:, t, :], top[:, 3:4], None, ALU.is_gt))
                ts(eqs[:, t, :], lgt[:, t, :], top[:, 3:4], None, ALU.is_equal)
                link(v.tensor_reduce(flag[:, t:t + 1], sel[:, t, :], AX, ALU.add))
                ts(flag[:, 2 + t:3 + t], flag[:, t:t + 1], -1.0, float(TOPK), ALU.mult, ALU.add)
                link(v.tensor_tensor_scan(cnt[:, t, :], eqs[:, t, :], zer, 0.0, ALU.add, ALU.add))
                link(ts(tie[:, t, :], cnt[:, t, :], flag[:, 2 + t:3 + t], None, ALU.is_le))
                link(tt(tie[:, t, :], tie[:, t, :], eqs[:, t, :], ALU.mult))
                tt(sel[:, t, :], sel[:, t, :], tie[:, t, :], ALU.add).then_inc(S("sel_ready"), 1)
                ts(top[:, 7:8], top[:, 0:1], -1.0, None, ALU.mult).then_inc(S("top_ready"), 1)

            stages = {"vec": vec, "normx": normx, "angle": angle, "normm": normm, "kk_raw": kk_raw, "rz": rz, "kk": kkn, "bonus": bonus, "tilde": tilde,
                      "ck": ck, "cq": cq, "attn_s": attn_s, "attn_t": attn_t, "gates": gates, "L": L, "inv_a": inv,
                      "inv_b": inv_b, "aq": lambda g: az("aq", g), "ak": lambda g: az("ak", g), 
                      "seq": seq, "gn": gn, "gn2": gn2, "wo": wo}
            for st, arg in ORDER:
                if st in stages:
                    stages[st](arg)

            def one_hot(e):
                for t in range(NT):
                    ins = ts(G[:, t, :], cc("iota"), rank[:, t, bass.ds(e, 1)], None, ALU.is_equal)
                ins.then_inc(S("G_ready"), 1)

            turned_x(NT - 1)
            for t in range(NT):
                dve.wait_ge(S("rstd_ready"), NORMS.index(("ffn", t)) + 1)
                drained(dve, "wo", t, 1)
                ts(xn[:, t, :], x[:, t, :], rst[:, 4 + t:5 + t], None, ALU.mult).then_inc(S("xn_ready"), 1)
            ps = filled(dve, "b1")
            drain(v.tensor_copy(b1T, ps[:, :]), "b1")
            choose(NT - 1)
            for t in range(NT):
                ps = filled(dve, "rk", t)
                drain(stt(rank[:, t, 0:E], ps[:, 0:E], UNSEL, sel[:, t, :], ALU.add, ALU.mult), "rk")
                drained(dve, "rk", t)
                link(ts(rank[:, t, 0:E], rank[:, t, 0:E], -UNSEL, None, ALU.add))
            one_hot(0)
            for t in range(NT):
                dve.wait_ge(S("lexp_ready"), t + 1)
                link(tt(gate[:, t, 0:E], eqs[:, t, :], sel[:, t, :], ALU.mult))
                link(v.tensor_reduce(flag[:, t:t + 1], gate[:, t, 0:E], AX, ALU.add))
                link(v.reciprocal(flag[:, t:t + 1], flag[:, t:t + 1]))
                link(ts(gate[:, t, 0:E], gate[:, t, 0:E], flag[:, t:t + 1], None, ALU.mult))
                v.tensor_copy(Gw[:, t, :].rearrange("p (h c) -> p h c", h=2)[:, :, 0:E], rep(gate[:, t, 0:E], 2)).then_inc(S("gate_ready"), 1)
            v.tensor_reduce(flag[:, 3:4], EA[:, 2, 256:256 + 2 * (E + 1)], AX, ALU.max).then_inc(S("rmax_ready"), 1)
            dve.wait_ge(S("allmax_ready"), 1)
            link(ts(flag[:, 1:2], flag[:, 0:1], float(CAP) - 0.5, None, ALU.is_gt))
            v.tensor_copy(flagi[:, :], flag[:, 1:2]).then_inc(S("flag_ready"), 1)

            def gathered(n):
                dve.wait_ge(S("xg_filled"), n + 1)
                tt(xgT, XG[:, :].rearrange("p (k c) -> p k c", c=CAP), each(vcol("norm_ffn", 0, KC), CAP),
                   ALU.mult).then_inc(S("xg_evac"), 1)

            def add_back(q, t):
                for half in range(2):
                    s = slice(half * W, (half + 1) * W)
                    dve.wait_ge(S("c_filled"), 4 * q + 2 * t + half + 1)
                    tt(x[:, t, s], x[:, t, s], (C0, C1)[half][:, :], ALU.add).then_inc(S("c_added"), 1)

            def expert(e, g, j, n):
                k = GROUP * g + j

                def own(ins, i):
                    ins.then_inc(S("expert_step"), 1)
                    dve.wait_ge(S("expert_step"), 4 * k + i)

                reached(dve, "gt_filled", k)
                for t in range(NT):
                    ins = ts(Gw[:, t, :].rearrange("p (h c) -> p h c", h=2), rep(cc("iota"), 2), rank[:, t, bass.ds(e, 1)], gate[:, t, bass.ds(e, 1)],
                             ALU.is_equal, ALU.mult)
                ins.then_inc(S("Gw_ready"), 1)
                dve.wait_ge(S("xg_filled"), n + 1)
                one_hot(e + 1)
                add_back(n, 0)

                def biased(dst, bank, i):
                    bias = b1T[:, bass.ds(e * 16 + 8 * i, 8)].rearrange("p (h b) -> p b h", b=4)
                    return tt(dst.rearrange("p (b h c) -> p b h c", h=2, c=CAP),
                              bank[:, :].rearrange("p (b h c) -> p b h c", h=2, c=CAP),
                              bias.unsqueeze(3).to_broadcast([P, 4, 2, CAP]), ALU.add)

                dve.wait_ge(S("tu_filled"), 2 * k + 1)
                own(biased(glu, TU, 0), 1)
                ts(glu, glu, LIMIT, None, ALU.min).then_inc(S("glu_ready"), 1)
                dve.wait_ge(S("tu_filled"), 2 * k + 2)
                own(biased(lin, U0, 1), 2)
                own(ts(lin, lin, LIMIT, -LIMIT, ALU.min, ALU.max), 3)
                own(stt(lin, lin, 1.0, glu, ALU.add, ALU.mult), 4)
                dve.wait_ge(S("sig_ready"), k + 1)
                products(dve, g, j - 1, 5) if j else products(dve, g - 1, GROUP - 1, 5)
                tt(actT, lin, sig, ALU.mult).then_inc(S("act_ready"), 1)
                gathered(n + 1)
                add_back(n, 1)

            def serve(r):
                if not isinstance(r, int):
                    dve.wait_ge(S("Gw_ready"), r * E)
                    ts(EA[:, 2, 256:256 + 2 * (E + 1)], EA[:, 2, 256:256 + 2 * (E + 1)], -float(CAP), None,
                       ALU.add).then_inc(S("rank_shifted"), 1)
                    dve.wait_ge(S("rank_shifted"), r)
                    v.memset(ysb, 0.0).then_inc(S("y_evac"), 1)
                    v.memset(GTw, 0.0).then_inc(S("gt_evac"), 1)
                    dve.wait_ge(S("xg_filled"), r * (E + 1))
                    one_hot(0)
                else:
                    v.engine_nop().then_inc(S("y_evac"), 1)
                gathered(r * (E + 1))
                if isinstance(r, int):
                    dve.wait_ge(S("gate_turned"), 1)
                for j in range(GROUP):
                    expert(j, r * QUADS, j, r * (E + 1) + j)
                with dve.Fori(1, QUADS) as g:
                    for j in range(GROUP):
                        expert(GROUP * g + j, r * QUADS + g, j, r * (E + 1) + GROUP * g + j)
                for t in range(NT):
                    add_back(r * (E + 1) + E, t)

            serve(0)
            dve.wait_ge(S("flag_ready"), 1)
            more = dve.value_load(flagi[0:1, 0:1], min_val=0, max_val=1)
            with dve.If(more > 0):
                with dve.Fori(1, T // CAP) as r:
                    serve(r)
            v.engine_nop().then_inc(S("all_added"), 1)

        @block.scalar
        def _(act):
            a = nc.scalar

            def drain(ins, kind):
                ins.then_inc(Drained(kind), 1)

            def copy(o, i):
                return a.activation(o, i, ACT.Copy)

            act.dma_start(ident, A["consts"][:, 0:P]).then_inc(S("ident_landed"), 16)
            for name in list(ROWS)[0::2]:
                act.dma_start(row_tile(name), row_source(name)).then_inc(S("rows_landed"), 16)
            act.dma_start(posi[:, :], A["positions"].rearrange("o (t p) -> p (o t)", p=P), allow_slow_non_contiguous=True).then_inc(S("pos_landed"), 16)

            def squares(name, i, n, src, junk, wait=True):
                if NORMS.index(name):
                    act.wait_ge(S("squares_ready"), NORMS.index(name))
                for j in range(n):
                    ins = a.activation(junk(j), src(j), ACT.Square, accum_out=ssq[:, i + j:i + j + 1])
                ins.then_inc(S("squares_ready"), 1)

            def vec(_):
                pass

            def normx(_):
                act.wait_ge(S("x_landed"), 16)
                squares("x", 0, NT, lambda t: x[:, t, :], lambda t: A1[:, 3 + t, :])
                act.dma_start(const[:, P:NCONST], A["consts"][:, P:NCONST]).then_inc(S("const_landed"), 16)
                for i, name in enumerate(("a_q_gain", "a_k_gain", "c_q_gain", "c_k_gain")):
                    act.dma_start(gains[:, i, :], A[name].to_broadcast([P, HD])).then_inc(S("gains_landed"), 16)
                act.dma_start(w2a[0:64, :], A["r_w2"][0]).then_inc(S("lora_landed"), 16)
                act.dma_start(w2a[64:128, :], A["r_a2"][0]).then_inc(S("lora_landed"), 16)
                act.dma_start(g2w, A["r_g2"][0]).then_inc(S("lora_landed"), 16)

            def angle(_):
                act.wait_ge(S("mem_landed"), 16)
                squares("mem", 2, NT, lambda t: memx[:, t, :], lambda t: A1[:, 3 + t, :])
                act.wait_ge(S("angle_ready"), 1)
                rs = A1[:, 5, 128:128 + NT * HALF].rearrange("p (t k) -> p t k", t=NT)
                rc = A1[:, 5, 192:192 + NT * HALF].rearrange("p (t k) -> p t k", t=NT)
                a.activation(trig[:, :, 0:HALF], rc, ACT.Sin)
                a.activation(trig[:, :, HALF:ROT], rc, ACT.Sin)
                a.activation(trig[:, :, ROT:ROT + HALF], rs, ACT.Sin, scale=-1.0)
                a.activation(trig[:, :, ROT + HALF:2 * ROT], rs, ACT.Sin).then_inc(S("trig_ready"), 1)

            dst_rz = [ch(r_), ch(k_), ch(v_), wag]

            def rz(i):
                if i == 0:
                    act.wait_ge(S("omm_ready"), 1)
                for c in range(4 if i < 3 else 2):
                    n = 4 * i + c
                    ps = filled(act, "rz", n)
                    a.activation(dst_rz[i][:, c, :], ps[:, 0:T], ACT.Copy, scale=omm[:, n:n + 1]).then_inc(S("rz_scaled"), 1)

            def lora(_):
                drained(act, "rz", 13)
                a.activation(wag[0:64, 0, :], wag[0:64, 0, :], ACT.Tanh).then_inc(S("wlo_ready"), 1)
                a.activation(wag[:, 1, :], wag[:, 1, :], ACT.Sigmoid).then_inc(S("wlo_ready"), 1)
                for p in range(PAIRS):
                    ps = filled(act, "lw", p)
                    drain(a.activation(ch(sgw)[:, p, :], ps[:, 0:T], ACT.Sigmoid, bias=vcol("r_w0", p)), "lw")
                    ps = filled(act, "la", p)
                    drain(a.activation(ch(a_)[:, p, :], ps[:, 0:T], ACT.Sigmoid, bias=vcol("r_a0", p)), "la")
                    ps = filled(act, "lg", p)
                    drain(copy(ch(g_)[:, p, :], ps[:, 0:T]), "lg")

            def head_squares(kind, idx, name, col):
                ps = filled(act, kind, *idx)
                squares(name, col, HEADS, lambda h: ps[:, h * HD:(h + 1) * HD], lambda h: ajunk[:, h * HD:(h + 1) * HD])

            def ck(_):
                for t in range(NT):
                    head_squares("ck", (t,), ("ck", t), 8 + 4 * t)

            def kkn(_):
                for half in range(2):
                    ps = filled(act, "kn", half)
                    drain(a.activation(tmp7[:, half * W:(half + 1) * W], ps[:, :], ACT.Sqrt), "kn")

            def cv(_):
                for t in range(NT):
                    ps = filled(act, "cv", t)
                    drain(copy(vv[:, t, :], ps[:, :]), "cv")

            def evac_T(kind, idx, dst):
                t = idx[-1]
                ps = filled(act, kind, *idx)
                drain(copy(dst[:, :, t * P:(t + 1) * P], ps[:, :].rearrange("p (h k) -> p h k", k=P)), kind)

            def cq(_):
                for t in range(NT):
                    head_squares("cq", (t,), ("cq", t), 16 + 4 * t)

            def ckq_T(_):
                for t in range(NT):
                    evac_T("ckT", (t,), kT)
                for t in range(NT):
                    evac_T("cqT", (t,), qT)

            def tilde(_):
                act.wait_ge(S("pml_ready"), 1)
                act.wait_ge(S("cum_ready"), 1)
                a.activation(sgw, sgw, ACT.Exp, scale=LOGC).then_inc(S("exps_ready"), 1)
                a.activation(eN, cum, ACT.Exp, scale=-LOGC).then_inc(S("exps_ready"), 1)
                act.wait_ge(S("exps_ready"), 2)
                a.activation(cum, cum, ACT.Exp, scale=LOGC).then_inc(S("exps_ready"), 1)

            def attn_s(g):
                n_at = ORDER_ATTN.index(g)
                if g < NG:
                    for kind, dst in (("aqT", qT), ("akT", kT)):
                        for t in range(NT):
                            evac_T(kind, (g, t), dst)
                for t in range(NT):
                    pr_, _ = prob(g, t)
                    act.wait_ge(S("max_ready"), NT * n_at + t + 1)
                    if g not in (0, NG):
                        a.activation(mx[:, 5, t, :], mx[:, 4, t, :], ACT.Exp)
                    for h in range(HEADS):
                        ins = a.activation(pr_[:, h, :], pr_[:, h, :], ACT.Exp, bias=mx[:, 2, t, h:h + 1],
                                           accum_out=lsum[:, 1, t, h:h + 1])
                    ins.then_inc(S("probs_ready"), 1)

            def attn_t(g):
                for t, part, h0, nh, nk, k0 in tile_parts(g):
                    _, pt = prob(g, t)
                    ps = filled(act, "pT", g, t, part)
                    drain(copy(pt[:, h0:h0 + nh, :, :].rearrange("p h b k -> p (h b k)"), ps[:, 0:nh * nk]), "pT")
                if g == NG:
                    outs(1)

            def outs(n):
                for t in range(NT):
                    ps = filled(act, "oT", n, t)
                    if n == 2:
                        act.wait_ge(S("pj_filled"), ledger[("pj", (1, KC - 1))][1])
                    drain(copy(yT[:, :, t * P:(t + 1) * P], ps[:, :].rearrange("p (h k) -> p h k", k=P)), "oT")

            def gates(part):
                b, i = part
                n0 = ORDER_GATES.index(b) * KC
                for c in (2 * i, 2 * i + 1):
                    ps = filled(act, "gz", b, c)
                    if c >= 2 or n0:
                        act.wait_ge(S("pj_drained"), n0 + c - 1)
                    drain(a.activation(sg[c % 2], ps[:, 0:T], ACT.Sigmoid, bias=vcol("b_gate", 8 * b + c)), "gz")

            def tok(_):
                for kind, dst in (("vt", Vt), ("kt", Kt), ("bt", Bt)):
                    for half in range(2):
                        ps = filled(act, kind, half)
                        drain(copy(dst[:, half * W:(half + 1) * W], ps[:, :]), kind)

            def az(kind, g):
                i = ("aq", "ak").index(kind)
                for t in range(NT):
                    head_squares(kind, (g, t), ("qk"[i:i + 1], g, t), 24 + 16 * g + 8 * i + 4 * t)

            def av(g):
                for t in range(NT):
                    ps = filled(act, "av", g, t)
                    drain(copy(vv[:, t, :], ps[:, :]), "av")

            def inv(l):
                if l:
                    for half in range(2):
                        ps = filled(act, "iT", l, half)
                        drain(copy(Tm[:, half * W:(half + 1) * W], ps[:, :]), "iT")

            def gn2(_):
                drained(act, "gv", 1)
                a.activation(gnr, gnr, ACT.Sqrt).then_inc(S("gn_root"), 1)

            stages = {"vec": vec, "normx": normx, "angle": angle, "rz": rz, "lora": lora, "kk": kkn, "ck": ck, "cv": cv, "cq": cq,
                      "ckq_T": ckq_T, "tilde": tilde, "attn_s": attn_s, "attn_t": attn_t, "outA": lambda _: outs(2), "gates": gates,
                      "tok": tok, "av": av, "inv_a": inv, "aq": lambda g: az("aq", g), "ak": lambda g: az("ak", g), "gn2": gn2}
            for st, arg in ORDER:
                if st in stages:
                    stages[st](arg)
            for t in range(NT):
                for half in range(2):
                    drained(act, "wo", t, half)
                squares(("ffn", t), 4 + t, 1, lambda j: x[:, t, :], lambda j: EA[:, 4 + t, :])
            for t in range(NT):
                act.wait_ge(S("top_ready"), t + 1)
                a.activation(eqs[:, t, :], lgt[:, t, :], ACT.Exp, bias=small[:, t, 7:8]).then_inc(S("lexp_ready"), 1)

            def expert(g, j, n):
                k = GROUP * g + j
                for i, bank in enumerate((U0, U1)):
                    products(act, g, j, 2 * i + 1)
                    reached(act, "tu_filled", 2 * k)
                    copy(usb[:, i * W:(i + 1) * W], bank[:, :]).then_inc(S("u_evac"), 1)
                act.wait_ge(S("glu_ready"), k + 1)
                a.activation(sig, glu, ACT.Sigmoid, scale=ALPHA).then_inc(S("sig_ready"), 1)
                act.wait_ge(S("gt_filled"), k + 1)
                act.wait_ge(S("c_filled"), 4 * n + 4)
                copy(GTw, GB[:, 0:T]).then_inc(S("gt_evac"), 1)
                products(act, g, j, 5)
                copy(ysb, YB[:, :]).then_inc(S("y_evac"), 1)

            def serve(r):
                if isinstance(r, int):
                    act.wait_ge(S("gate_turned"), 1)
                    copy(GTw, GB[:, 0:T]).then_inc(S("gt_evac"), 1)
                for j in range(GROUP):
                    expert(r * QUADS, j, r * (E + 1) + j)
                with act.Fori(1, QUADS) as g:
                    for j in range(GROUP):
                        expert(r * QUADS + g, j, r * (E + 1) + GROUP * g + j)

            serve(0)
            act.wait_ge(S("flag_ready"), 1)
            more = act.value_load(flagi[0:1, 0:1], min_val=0, max_val=1)
            with act.If(more > 0):
                with act.Fori(1, T // CAP) as r:
                    serve(r)

        @block.gpsimd
        def _(pool):
            g = nc.gpsimd
            g.memset(negh[:, :], -0.5).then_inc(S("pool_const"), 1)
            pool.wait_ge(S("pool_const"), 1)
            norm_no = [0]

            def root(col, n, width):
                norm_no[0] += 1
                i = norm_no[0]
                pool.wait_ge(S("squares_ready"), i)
                g.tensor_scalar(ssq[:, col:col + n], ssq[:, col:col + n], 1.0 / width, EPS, ALU.mult, ALU.add).then_inc(S("mean_ready"), 1)
                pool.wait_ge(S("mean_ready"), i)
                g.tensor_tensor(rst[:, col:col + n], ssq[:, col:col + n], negh[:, 0:n], ALU.pow).then_inc(S("rstd_ready"), 1)

            def normx(_):
                root(0, NT, D)

            def angle(_):
                root(2, NT, D)

            def ck(_):
                for t in range(NT):
                    root(8 + 4 * t, HEADS, HD)

            def cq(_):
                for t in range(NT):
                    root(16 + 4 * t, HEADS, HD)

            def kk_raw(_):
                for half in range(2):
                    s = slice(half * W, (half + 1) * W)
                    pool.wait_ge(S("kk_raw"), half + 1)
                    g.tensor_tensor(tmp6[:, s], kk[:, s], kk[:, s], ALU.mult).then_inc(S("kksq_ready"), 1)

            def kkn(_):
                pool.wait_ge(S("cum_ready"), 1)
                g.tensor_tensor(sgw, cum, sgw, ALU.subtract).then_inc(S("pml_ready"), 1)

            def tilde(_):
                pool.wait_ge(S("exps_ready"), 3)
                g.tensor_copy(ePT[:, :, :], cum.rearrange("p (a c t) -> p a c t", c=NCH, t=CH)[:, :, :, CH - 1]).then_inc(S("ept_ready"), 1)

            def rotate(z, t):
                rot_no[0] += 1
                n = rot_no[0]
                z3 = z[:, t, :].rearrange("p (h k) -> p h k", k=HD)
                cos, sin = trig[:, t, 0:ROT], trig[:, t, ROT:2 * ROT]
                b0, b1 = rotb[:, 0, :, :], rotb[:, 1, :, :]
                if n > 1:
                    pool.wait_ge(S("rot_done"), n - 1)
                g.tensor_tensor(b0, z3[:, :, 0:ROT], rep(cos, HEADS), ALU.mult)
                g.tensor_tensor(b1[:, :, 0:HALF], z3[:, :, HALF:ROT], rep(sin[:, 0:HALF], HEADS), ALU.mult)
                g.tensor_tensor(b1[:, :, HALF:ROT], z3[:, :, 0:HALF], rep(sin[:, HALF:ROT], HEADS), ALU.mult).then_inc(S("rot_parts"), 1)
                pool.wait_ge(S("rot_parts"), n)
                g.tensor_tensor(z3[:, :, 0:ROT], b0, b1, ALU.add).then_inc(S("rot_done"), 1)

            rot_no = [0]

            def az(kind, gr):
                if gr == 0:
                    pool.wait_ge(S("trig_ready"), 1)
                i = ("aq", "ak").index(kind)
                for t in range(NT):
                    root(24 + 16 * gr + 8 * i + 4 * t, HEADS, HD)
                for t in range(NT):
                    drained(pool, kind, gr, t)
                    rotate((zq, zk)[i], t)

            def level(l):
                for half in range(2):
                    s = slice(half * W, (half + 1) * W)
                    if l == 0:
                        drained(pool, "lab", half)
                    else:
                        filled(pool, "iT" if l > 1 else "iZ", l - 1, half)
                        if l == 1:
                            pool.wait_ge(S("xt_ready"), half + 1)
                    mask = cc("level")[:, l * CH:(l + 1) * CH]
                    g.tensor_tensor(mm64(Lm[:, s]), mm64(LabT[:, s]), rep(mask, 8), ALU.mult).then_inc(S("level_ready"), 1)

            def inv(l):
                if l == 0:
                    level(0)
                if l + 1 < LEVELS:
                    level(l + 1)
                else:
                    pool.wait_ge(S("iT_filled"), ledger[("iT", (l, 1))][1])
                    g.memset(stS[0], 0.0).then_inc(S("state_zero"), 1)

            stages = {"normx": normx, "angle": angle, "kk_raw": kk_raw, "ck": ck, "cq": cq, "kk": kkn, "tilde": tilde, "aq": lambda g: az("aq", g), "ak": lambda g: az("ak", g), "inv_a": inv}
            for st, arg in ORDER:
                if st in stages:
                    stages[st](arg)
            pool.wait_ge(S("yb_ready"), 1)
            g.memset(EA[:, 2, 256:512], -UNSEL)
            g.memset(Gw, 0.0)
            g.memset(ysb, 0.0)
            g.memset(zer, 0.0).then_inc(S("zero_ready"), 1)
            for t in range(NT):
                root(4 + t, 1, D)
            pool.wait_ge(S("rmax_ready"), 1)
            g.partition_all_reduce(flag[:, 0:1], flag[:, 3:4], P, bass.bass_isa.ReduceOp.max).then_inc(S("allmax_ready"), 1)

        @block.sync
        def _(sp):
            sp.dma_start(x[:, :, :], A["x"].rearrange("o (t p) n -> p (o t) n", p=P)).then_inc(S("x_landed"), 16)
            for name in list(ROWS)[1::2]:
                sp.dma_start(row_tile(name), row_source(name)).then_inc(S("rows_landed"), 16)
            w_in, w_b, w_o, w_kv = A["w_in"][0], A["w_branch"][0], A["w_out"][0], A["w_mem_kv"][0]

            def source(kind, i):
                cols = {"r": OFF_R + W * i, "cq": OFF_CQ, "aq": W * i, "ak": A_COLS + W * i, "av": 2 * A_COLS + W * i,
                        "g0": OFF_GATE + D * i, "g1": OFF_GATE + D * i + W}
                if kind in cols:
                    c = cols[kind]
                    return w_in[:, c:c + (256 if (kind, i) == ("r", 3) else W)]
                if kind == "wb":
                    return w_b[i]
                if kind == "wo":
                    return w_o[:, W * i:W * (i + 1)]
                return w_kv[:, 0:W] if kind == "mk" else w_kv[:, W:2 * W]

            def load_piece(e, g, j, s):
                i = piece_slot(j, s)
                w1 = A["exp_w1"][0, bass.ds(e, 1), :, :].rearrange("o (k p) n -> p (o k) n", p=P)
                w2 = A["exp_w2"][0, bass.ds(e, 1), :, :].rearrange("o (k p) n -> p (o k) n", p=P)
                reached(sp, f"slot_used{i}", piece_no(g, j, s))
                src, n = (w1[:, :, s * W:(s + 1) * W], W) if s < 4 else (w2[:, 4 * (s - 4):4 * (s - 3), :], D)
                sp.dma_start(slots[i].rearrange("p (k n) -> p k n", n=n), src).then_inc(S(f"slot_landed{i}"), 16)

            last_use = last_filled
            for n, (kind, i) in enumerate(loads):
                if n >= RING:
                    k2, idx = last_use(loads[n - RING])
                    filled(sp, k2, *idx)
                if n == len(loads) - 1:
                    drained(sp, "oT", 2, NT - 1)
                    load_piece(1, 0, 1, 0)
                if n == 2:
                    sp.dma_start(memx, A["mem"].rearrange("o (t p) n -> p (o t) n", p=P)).then_inc(S("mem_landed"), 16)
                src = source(kind, i)
                rows_, cols_ = src.shape
                dst = ring[:, n % RING, 0:rows_ // P * cols_].rearrange("p (k n) -> p k n", n=cols_)
                sp.dma_start(dst, src.rearrange("(k p) n -> p k n", p=P)).then_inc(S(f"slot_landed{n % RING}"), 16)
            sp.wait_ge(S("zero_ready"), 1)
            for half, s in enumerate((0, CAP)):
                sp.dma_start(ysb[s:s + E, :], A["exp_b2"][0, :, half * W:(half + 1) * W]).then_inc(S("late_landed"), 16)
            sp.dma_start(b1raw.rearrange("p (q f) -> p q f", f=P),
                         A["exp_b1"][0].rearrange("e (c f) -> (e c) f", f=P).rearrange("(q p) f -> p q f", p=P)).then_inc(S("late_landed"), 16)
            sp.dma_start(rw, A["router_w"][0].rearrange("(k p) e -> p k e", p=P)).then_inc(S("late_landed"), 16)
            sp.dma_start(rbias, A["router_b"].to_broadcast([P, E])).then_inc(S("late_landed"), 16)

            filled(sp, "pj", 0, KC - 1)
            for m in (7, 0, 3, 4, 5, 1, 2):
                if m < RING:
                    k2, idx = last_use(loads[[i for i in range(len(loads)) if i % RING == m][-1]])
                    filled(sp, k2, *idx)
                load_piece(m // PIECES, 0, m // PIECES, m % PIECES)
            for m in range(SLOTS, GROUP * PIECES):
                load_piece(m // PIECES, 0, m // PIECES, m % PIECES)

            def load_groups(r, first):
                with sp.Fori(first, QUADS) as g:
                    for m in range(GROUP * PIECES):
                        load_piece(GROUP * g + m // PIECES, r * QUADS + g, m // PIECES, m % PIECES)

            load_groups(0, 1)
            sp.wait_ge(S("flag_ready"), 1)
            more = sp.value_load(flagi[0:1, 0:1], min_val=0, max_val=1)
            with sp.If(more > 0):
                with sp.Fori(1, T // CAP) as r:
                    load_groups(r, 0)
            sp.wait_ge(S("all_added"), 1)
            sp.dma_start(out.rearrange("o (t p) n -> p (o t) n", p=P), x[:, :, :]).then_inc(S("out_written"), 16)
            sp.wait_ge(S("out_written"), 16)


ORDER_ATTN = [a for s, a in ORDER if s == "attn_s"]
ORDER_GATES = [a[0] for s, a in ORDER if s == "gates" and a[1] == 0]


def last_filled(load):
    kind, i = load
    if kind == "r":
        return "rz", ((3, 7, 11, 13)[i],)
    if kind in ("mk", "mv", "cq"):
        return {"mk": "ck", "mv": "cv", "cq": "cq"}[kind], (NT - 1,)
    if kind in ("aq", "ak", "av"):
        return kind, (i, NT - 1)
    if kind == "wo":
        return "wo", (NT - 1, i)
    if kind == "wb":
        return "pj", (i, KC - 1)
    return "gz", (i, 3 if kind == "g0" else 7)


def shape_constants():
    p = np.arange(P)[:, None]
    c = np.zeros((P, NCONST), np.float32)

    def put(name, val):
        a, n = CONST[name]
        c[:, a:a + n] = val

    j = np.arange(P)[None, :]
    put("ident", p == j)
    put("jblk", p // RD == j // RD)
    am = []
    for window, dil in GROUPS:
        same = (p - j) % dil == 0
        span = window // dil
        am.append(np.where(same & ((P + p - j) <= span * dil), 0, NEG))
        am.append(np.where(same & (j <= p) & ((p - j) <= span * dil), 0, NEG))
    put("amask", np.concatenate(am, 1))
    s, t = np.arange(P)[:, None] % CH, np.arange(CH)[None, :]
    put("strict", t > s)
    put("incl", t >= s)
    put("level", np.concatenate([(s >> (i + 1) == t >> (i + 1)) & ((t >> i) & 1 == 1) & ((s >> i) & 1 == 0)
                                 for i in range(LEVELS)], 1))
    put("eye", s == t)
    put("reset", (np.arange(T) % CH != 0)[None, :])
    put("earlier", p < j)
    put("ones", 1.0)
    put("iota", np.arange(CAP)[None, :])
    put("invf", np.float32(THETA) ** (-np.arange(HALF, dtype=np.float32) / np.float32(HALF)))
    return c


NAMES = ["x", "mem", "positions", "norm_mix", "w_in", "b_gate", "a_q_gain", "a_k_gain", "r_mu", "r_w0", "r_w2", "r_a0",
         "r_a2", "r_g2", "r_k_k", "r_k_a", "r_r_k", "r_ln_w", "r_ln_b", "mem_norm", "w_mem_kv", "c_q_gain", "c_k_gain",
         "w_branch", "w_out", "norm_ffn", "router_w", "router_b", "exp_w1", "exp_b1", "exp_w2", "exp_b2"]


def kernel(**inputs):
    import concourse.bacc as bacc
    from concourse.bass_utils import run_bass_kernel_spmd

    nc = bacc.Bacc("TRN2", target_bir_lowering=False, num_devices=1)
    arrays = {f"in_{n}": np.ascontiguousarray(inputs[n]) for n in NAMES}
    arrays["in_consts"] = shape_constants()
    aps = {n[3:]: nc.dram_tensor(n, a.shape, mybir.dt.from_np(a.dtype), kind="ExternalInput").ap()
           for n, a in arrays.items()}
    out = nc.dram_tensor("out", (1, T, D), F32, kind="ExternalOutput").ap()
    build(nc, aps, out)
    r = run_bass_kernel_spmd(nc, [arrays], core_ids=[0])
    return r.results[0]["out"]
```
